# Optimizing a Trainium2 kernel written in Bass

```python
import jax, jax.numpy as jnp
from jax import lax
import numpy as np

D_MODEL = 1024
BATCH = 1
SEQ = 256
DEPTH = 1

PLE_DIM = 256
GLA_HEADS = 4
GLA_DK = 64
GLA_DV = 128
GLA_LOWRANK = 16
GLA_TAU = 16.0
GLA_CHUNK = 64
MOBA_HEADS = 4
MOBA_HD = 128
MOBA_BLOCK = 256
MOBA_TOPK = 3
MOBA_QBLOCK = 128
ROPE_THETA = 10000.0
D_FF = 4 * D_MODEL
EPS = 1e-6

GLA_QK_W = GLA_HEADS * GLA_DK
GLA_V_W = GLA_HEADS * GLA_DV
MOBA_W = MOBA_HEADS * MOBA_HD
MIX_W = GLA_V_W + MOBA_W
SPLIT_SIZES = (GLA_QK_W, GLA_QK_W, GLA_V_W, GLA_V_W, GLA_LOWRANK, MOBA_W, MOBA_W, MOBA_W)
IN_W = 2 * GLA_QK_W + 2 * GLA_V_W + GLA_LOWRANK + 3 * MOBA_W

kernel_name = "hymba_gla_moba_sqrelu_ple"

def rms_norm(x, g):
    xf = x.astype(jnp.float32)
    y = xf * lax.rsqrt(jnp.mean(xf * xf, axis=-1, keepdims=True) + EPS)
    return (y * g.astype(jnp.float32)).astype(x.dtype)

def rope(x, positions):
    hd = x.shape[-1]
    half = hd // 2
    inv = 1.0 / (ROPE_THETA ** (jnp.arange(half, dtype=jnp.float32) / half))
    ang = positions.astype(jnp.float32)[:, None, :, None] * inv
    cos, sin = jnp.cos(ang), jnp.sin(ang)
    xf = x.astype(jnp.float32)
    x1, x2 = xf[..., :half], xf[..., half:]
    out = jnp.concatenate([x1 * cos - x2 * sin, x2 * cos + x1 * sin], axis=-1)
    return out.astype(x.dtype)

def gla_chunked(q, k, v, log_a):
    B, H, S, dk = q.shape
    dv = v.shape[-1]
    C = GLA_CHUNK
    nc = S // C
    q = q.reshape(B, H, nc, C, dk)
    k = k.reshape(B, H, nc, C, dk)
    v = v.reshape(B, H, nc, C, dv)
    g = log_a.reshape(B, H, nc, C, dk)
    b = jnp.cumsum(g, axis=3)
    b_last = b[:, :, :, -1:, :]
    q_dec = q * jnp.exp(b) * (dk ** -0.5)
    k_inv = k * jnp.exp(-b)
    causal = jnp.tril(jnp.ones((C, C), dtype=bool))
    A = jnp.einsum('bhncd,bhnjd->bhncj', q_dec, k_inv)
    A = jnp.where(causal, A, 0.0)
    o_intra = jnp.einsum('bhncj,bhnje->bhnce', A, v)
    k_to_end = k * jnp.exp(b_last - b)
    dS = jnp.einsum('bhncd,bhnce->bhnde', k_to_end, v)
    decay = jnp.exp(b_last[:, :, :, 0, :])

    def step(state, inp):
        ds_n, dec_n = inp
        return dec_n[..., None] * state + ds_n, state

    _, s_prev = lax.scan(step, jnp.zeros((B, H, dk, dv), jnp.float32),
                         (jnp.moveaxis(dS, 2, 0), jnp.moveaxis(decay, 2, 0)))
    s_prev = jnp.moveaxis(s_prev, 0, 2)
    o_inter = jnp.einsum('bhncd,bhnde->bhnce', q_dec, s_prev)
    return (o_intra + o_inter).reshape(B, H, S, dv)

def moba_attention(q, k, v):
    B, H, S, hd = q.shape
    BLK = MOBA_BLOCK
    QB = MOBA_QBLOCK
    nb = -(-S // BLK)
    pad = nb * BLK - S
    k_p = jnp.pad(k, ((0, 0), (0, 0), (0, pad), (0, 0)))
    v_p = jnp.pad(v, ((0, 0), (0, 0), (0, pad), (0, 0)))
    k_blocks = k_p.reshape(B, H, nb, BLK, hd)
    v_blocks = v_p.reshape(B, H, nb, BLK, hd)
    k_mean = jnp.mean(k_blocks.astype(jnp.float32), axis=3)
    n_sel = min(MOBA_TOPK, nb)
    nqb = S // QB
    q_blocks = q.reshape(B, H, nqb, QB, hd).transpose(2, 0, 1, 3, 4)
    scale = hd ** -0.5
    bi = jnp.arange(B)[:, None, None, None]
    hi = jnp.arange(H)[None, :, None, None]
    blk_ids = jnp.arange(nb)

    def one_block(args):
        qb, i = args
        q_start = i * QB
        kb = q_start // BLK
        qf = qb.astype(jnp.float32)
        gate = jnp.einsum('bhqd,bhnd->bhqn', qf, k_mean)
        gate = jnp.where(blk_ids < kb, gate, -jnp.inf)
        _, idx = lax.top_k(gate, n_sel)
        sel_valid = idx < kb
        k_sel = k_blocks[bi, hi, idx].astype(jnp.float32)
        v_sel = v_blocks[bi, hi, idx].astype(jnp.float32)
        s_sel = jnp.einsum('bhqd,bhqnkd->bhqnk', qf, k_sel) * scale
        s_sel = jnp.where(sel_valid[..., None], s_sel, -jnp.inf).reshape(B, H, QB, n_sel * BLK)
        k_own = lax.dynamic_index_in_dim(k_blocks, kb, axis=2, keepdims=False).astype(jnp.float32)
        v_own = lax.dynamic_index_in_dim(v_blocks, kb, axis=2, keepdims=False).astype(jnp.float32)
        s_own = jnp.einsum('bhqd,bhkd->bhqk', qf, k_own) * scale
        q_pos = q_start + jnp.arange(QB)
        k_pos = kb * BLK + jnp.arange(BLK)
        s_own = jnp.where(k_pos[None, :] <= q_pos[:, None], s_own, -jnp.inf)
        probs = jax.nn.softmax(jnp.concatenate([s_sel, s_own], axis=-1), axis=-1)
        p_sel = probs[..., :n_sel * BLK].reshape(B, H, QB, n_sel, BLK)
        p_own = probs[..., n_sel * BLK:]
        o = (jnp.einsum('bhqnk,bhqnkd->bhqd', p_sel, v_sel)
             + jnp.einsum('bhqk,bhkd->bhqd', p_own, v_own))
        return o.astype(q.dtype)

    out = lax.map(one_block, (q_blocks, jnp.arange(nqb)))
    return out.transpose(1, 2, 0, 3, 4).reshape(B, H, S, hd)

def setup_inputs(seed: int = 0) -> dict:
    key = jax.random.key(seed)
    ks = jax.random.split(key, 20)
    f32 = jnp.float32

    def nrm(k, shape, scale):
        return jax.random.normal(k, shape, f32) * scale

    def gain(k, shape):
        return 1.0 + 0.02 * jax.random.normal(k, shape, f32)

    L = DEPTH
    return {
        "x": nrm(ks[0], (BATCH, SEQ, D_MODEL), 1.0),
        "p": nrm(ks[1], (DEPTH, BATCH, SEQ, PLE_DIM), 1.0),
        "positions": jnp.broadcast_to(jnp.arange(SEQ, dtype=jnp.int32), (BATCH, SEQ)),
        "g_mix": gain(ks[2], (L, D_MODEL)),
        "w_in": nrm(ks[3], (L, D_MODEL, IN_W), D_MODEL ** -0.5),
        "w_gla_a2": nrm(ks[4], (L, GLA_LOWRANK, GLA_QK_W), GLA_LOWRANK ** -0.5),
        "b_gla_a": nrm(ks[5], (L, GLA_QK_W), 0.1),
        "g_gla_out": gain(ks[6], (L, GLA_DV)),
        "g_moba_q": gain(ks[7], (L, MOBA_HD)),
        "g_moba_k": gain(ks[8], (L, MOBA_HD)),
        "w_out": nrm(ks[9], (L, MIX_W, D_MODEL), MIX_W ** -0.5),
        "g_ffn": gain(ks[10], (L, D_MODEL)),
        "w_up": nrm(ks[11], (L, D_MODEL, D_FF), D_MODEL ** -0.5),
        "w_down": nrm(ks[12], (L, D_FF, D_MODEL), D_FF ** -0.5),
        "g_ple_gate": gain(ks[13], (L, D_MODEL)),
        "w_ple_gate": nrm(ks[14], (L, D_MODEL, D_MODEL), D_MODEL ** -0.5),
        "w_ple_proj": nrm(ks[15], (L, PLE_DIM, D_MODEL), PLE_DIM ** -0.5),
        "g_ple_emb": gain(ks[16], (L, D_MODEL)),
    }

def reference(x, p, positions, g_mix, w_in, w_gla_a2, b_gla_a, g_gla_out, g_moba_q, g_moba_k,
              w_out, g_ffn, w_up, w_down, g_ple_gate, w_ple_gate, w_ple_proj, g_ple_emb):
    B, S, _ = x.shape
    split_points = np.cumsum(SPLIT_SIZES)[:-1].tolist()

    def heads(t, n):
        return t.reshape(B, S, n, -1).transpose(0, 2, 1, 3)

    h = x
    for i in range(DEPTH):
        u = rms_norm(h, g_mix[i])
        z = u @ w_in[i]
        gq, gk, gv, gg, ga, mq, mk, mv = jnp.split(z, split_points, axis=-1)

        a_pre = (ga @ w_gla_a2[i] + b_gla_a[i]).astype(jnp.float32)
        log_a = jax.nn.log_sigmoid(a_pre) / GLA_TAU
        o_gla = gla_chunked(heads(gq, GLA_HEADS).astype(jnp.float32),
                            heads(gk, GLA_HEADS).astype(jnp.float32),
                            heads(gv, GLA_HEADS).astype(jnp.float32),
                            heads(log_a, GLA_HEADS))
        o_gla = rms_norm(o_gla, g_gla_out[i]).transpose(0, 2, 1, 3).reshape(B, S, GLA_V_W)
        o_gla = o_gla.astype(x.dtype) * jax.nn.silu(gg)

        q = rope(rms_norm(heads(mq, MOBA_HEADS), g_moba_q[i]), positions)
        k = rope(rms_norm(heads(mk, MOBA_HEADS), g_moba_k[i]), positions)
        v = heads(mv, MOBA_HEADS)
        o_moba = moba_attention(q, k, v).transpose(0, 2, 1, 3).reshape(B, S, MOBA_W)

        h = h + jnp.concatenate([o_gla, o_moba.astype(x.dtype)], axis=-1) @ w_out[i]

        f = rms_norm(h, g_ffn[i]) @ w_up[i]
        h = h + jnp.square(jax.nn.relu(f)) @ w_down[i]

        gate = jax.nn.sigmoid(rms_norm(h, g_ple_gate[i]) @ w_ple_gate[i])
        e = rms_norm(p[i] @ w_ple_proj[i], g_ple_emb[i])
        h = h + gate * e
    return h


_drawn_inputs = setup_inputs


def setup_inputs(seed=0):
    import zlib

    import numpy as np

    out = dict(_drawn_inputs(seed))
    spreads = {}
    factors = {'g_mix': 2.678,
     'b_gla_a': 3.147,
     'g_gla_out': 6.624,
     'g_moba_q': 8.0,
     'g_moba_k': 8.0,
     'g_ffn': 10.222,
     'g_ple_gate': 193.156,
     'g_ple_emb': 200.0}
    for name, (base, spread) in spreads.items():
        noise = np.random.default_rng([zlib.crc32(name.encode()), seed]).standard_normal(out[name].shape)
        drawn = base * np.exp(spread * noise) if base else spread * noise
        out[name] = __import__('jax').numpy.asarray(drawn.astype(out[name].dtype))
    for name, factor in factors.items():
        out[name] = (out[name] * factor).astype(out[name].dtype)
    return out
```

```python
import concourse.bass as bass
from concourse import mybir
from contextlib import ExitStack

F32 = mybir.dt.float32
F32R = mybir.dt.float32r
I32 = mybir.dt.int32
ACT = mybir.ActivationFunctionType
ALU = mybir.AluOpType
AXIS_X = mybir.AxisListType.X

P = 128
SEQ, D, D_FF, PLE = 256, 1024, 4096, 256
T = SEQ // P
KT = D // P
NW = 512
GROUPS = D_FF // NW
HEADS = 4
HD = 128
DK, DV = 64, 128
CHUNK = 64
LOWRANK = 16
TAU = 16.0
EPS = 1e-6
HALF = 1024
RAW, PAIRS = 4, 4
C_GQK, C_GV, C_GG, C_GA, C_MQ, C_MK, C_MV = 0, 512, 1024, 1536, 1552, 2064, 2576
GROUP_COLS = [C_MQ, C_MK, C_GQK, C_GG, C_GV, C_MV]
Z_MQ, Z_MK, Z_GQK, Z_GG, Z_GV, Z_MV = range(6)

H_PP = 4 * 5
H_GROUP = [0, 4, 8, 12, 16, H_PP + 2]
H_OUT = H_GROUP[5] + 4
H_UP0 = H_OUT + KT
H_LOOP = H_UP0 + 4
LOOP_HALVES = 8
H_DOWN_LAST = H_LOOP + LOOP_HALVES * (GROUPS - 1)
H_GATE = H_DOWN_LAST + 4
H_END = H_GATE + 8

TWO_PI = 6.283185307179586
PI_A = 6.28125
PI_B = 0.0019340515136719
PI_C = TWO_PI - PI_A - PI_B
ROUND = 12582912.0
HALF_PI = 1.5707963267948966
PI_BELOW = 3.1415925
MASKED = -1e30

T_BANK = [4, 4, 0]


def build(nc, x, p, positions, g_mix, w_in, w_a2, b_a, g_gla, g_mq, g_mk, w_out, g_ffn, w_up, w_down,
          g_gate, w_gate, w_pp, g_ple, inv_freq, out):
    ctx = ExitStack()
    with ctx:
        def sb(name, shape, dt=F32):
            return ctx.enter_context(nc.sbuf_tensor(name, shape, dt))

        def sem(name):
            return ctx.enter_context(nc.semaphore(name))

        w_raw = sb("w_raw", [P, RAW, 2 * HALF])
        w_hi = sb("w_hi", [P, PAIRS, HALF], F32R)
        w_lo = sb("w_lo", [P, PAIRS, HALF], F32R)
        act_hi = sb("act_hi", [P, KT, SEQ], F32R)
        act_lo = sb("act_lo", [P, KT, SEQ], F32R)
        mix_hi = sb("mix_hi", [P, KT, SEQ], F32R)
        mix_lo = sb("mix_lo", [P, KT, SEQ], F32R)
        act_f32 = sb("act_f32", [P, KT * SEQ])
        h = sb("h", [P, T, D])
        z = sb("z", [P, 6, T, NW])
        qk_T = sb("qk_T", [P, 2 * HEADS * SEQ])
        g_ple_b = sb("g_ple_b", [P, D])
        scratch = sb("scratch", [P, 4 * T * 256])
        la = sb("la", [P, T, 256])
        la_nabs = sb("la_nabs", [P, T, 256])
        dec = sb("dec", [P, T, 2, 256])
        inv_dec = sb("inv_dec", [P, T, 256])
        qd_T = sb("qd_T", [P, 2, T, P])
        ki_T = sb("ki_T", [P, 2, T, P])
        a_T = sb("a_T", [P, 2, T, 2, P])
        state = sb("state", [P, 3, 2, DV])
        decay = sb("decay", [P, 2, T, 2])
        rope_q = sb("rope_q", [P, 4, T, 64])
        rope_k = sb("rope_k", [P, 4, T, 64])
        sin_t = sb("sin_t", [P, T * 64])
        cos_t = sb("cos_t", [P, T * 64])
        angle = sb("angle", [P, T * 64])
        turns = sb("turns", [P, T * 64])
        p_sb = sb("p_sb", [P, T, PLE])
        p_hi = sb("p_hi", [P, 2, SEQ], F32R)
        p_lo = sb("p_lo", [P, 2, SEQ], F32R)
        ident = sb("ident", [P, P])
        tri = sb("tri", [P, P])
        rest = sb("rest", [P, P])
        chunk_sum = sb("chunk_sum", [P, 2])
        causal = sb("causal", [P, 2 * P])
        w_ga = sb("w_ga", [P, KT, LOWRANK])
        ga_T = sb("ga_T", [LOWRANK, SEQ])
        a2 = sb("a2", [LOWRANK, 256])
        b_a_b = sb("b_a_b", [P, 256])
        g_gla_b = sb("g_gla_b", [P, DV])
        g_mq_b = sb("g_mq_b", [P, HD])
        g_mk_b = sb("g_mk_b", [P, HD])
        inv_b = sb("inv_b", [P, 64])
        pos_i = sb("pos_i", [P, T], I32)
        pos_f = sb("pos_f", [P, T])
        gain_rows = sb("gain_rows", [24, P])
        gains = sb("gains", [P, 24])
        ss = sb("ss", [P, 8])
        rs = sb("rs", [P, 8])
        ms = sb("ms", [P, 8])
        nt = sb("nt", [P, 8])
        ss_q = sb("ss_q", [P, 8])
        rs_q = sb("rs_q", [P, 8])
        ss_k = sb("ss_k", [P, 8])
        rs_k = sb("rs_k", [P, 8])
        nq = sb("nq", [P, 8])
        qmax = sb("qmax", [P, 8])
        nbias = sb("nbias", [P, 8])
        rowsum = sb("rowsum", [P, 8])
        rinv = sb("rinv", [P, 8])
        ss_o = sb("ss_o", [P, 8])
        rs_o = sb("rs_o", [P, 8])
        one = sb("one", [P, 1])
        ps = ctx.enter_context(nc.psum_tensor("ps", [P, 8, NW], F32))

        probs = act_f32[:, 0:HEADS * 384].rearrange("p (h c) -> p h c", h=HEADS)
        squares = act_f32[:, 0:T * NW]
        act3 = act_f32[:, :].rearrange("p (k s) -> p k s", k=KT)
        q_T = qk_T[:, 0:HEADS * SEQ].rearrange("p (h s) -> p h s", h=HEADS)
        k_T = qk_T[:, HEADS * SEQ:].rearrange("p (h s) -> p h s", h=HEADS)
        e = qk_T[:, :].rearrange("p (t n) -> p t n", t=T)
        probs_T = z[:, Z_MQ:Z_MQ + 2, :, :].rearrange("p g t n -> p (g t n)")[:, 0:HEADS * 384].rearrange(
            "p (h c) -> p h c", h=HEADS)
        hidden = z[:, Z_MQ, :, :]
        o_gla = z[:, Z_GQK, :, :]
        gate_tmp = z[:, Z_MK:Z_MK + 2, :, :]
        rope_tmp = scratch[:, :].rearrange("p (i t h d) -> p i t h d", i=4, t=T, h=HEADS)
        o_squares = dec[:, :, :, :].rearrange("p t b n -> p (t b n)")
        silu_nabs = scratch[:, 0:T * NW]
        silu_log = scratch[:, T * NW:2 * T * NW]

        raw_ready = [sem(f"raw_ready{i}") for i in range(RAW)]
        hi_done, lo_done, half_used = sem("hi_done"), sem("lo_done"), sem("half_used")
        x_in, ga_in, p_in, a2_in, rows_in, pos_in, bc_in, ple_in = (
            sem(n) for n in ("x_in", "ga_in", "p_in", "a2_in", "rows_in", "pos_in", "bc_in", "ple_in"))
        consts = sem("consts")
        gains_T, gains_ready = sem("gains_T"), sem("gains_ready")
        x_T, xg_ready, act_hi_ready, act_lo_ready = sem("x_T"), sem("xg_ready"), sem("act_hi_ready"), sem("act_lo_ready")
        p_T, p_hi_ready, p_lo_ready = sem("p_T"), sem("p_hi_ready"), sem("p_lo_ready")
        ss_ready, ms_ready, rough_ready, rs_ready = sem("ss_ready"), sem("ms_ready"), sem("rough_ready"), sem("rs_ready")
        ga_done, ga_copied, apre_done = sem("ga_done"), sem("ga_copied"), sem("apre_done")
        neg_abs_ready, log1p_ready, la_ready = sem("neg_abs_ready"), sem("log1p_ready"), sem("la_ready")
        cums_done, decays_ready = sem("cums_done"), sem("decays_ready")
        z_ready = sem("z_ready")
        trig_arg, trig_ready, tables_ready, rope_high = sem("trig_arg"), sem("trig_ready"), sem("tables_ready"), sem("rope_high")
        sq_ready, msq_ready, rough_qk, qk_ready = sem("sq_ready"), sem("msq_ready"), sem("rough_qk"), sem("qk_ready")
        qkT_done, qkT_copied = sem("qkT_done"), sem("qkT_copied")
        gla_ops, glaT_done, glaT_copied = sem("gla_ops"), sem("glaT_done"), sem("glaT_copied")
        scores_done, masked, bias_ready, exp_done, probs_ready = (
            sem("scores_done"), sem("masked"), sem("bias_ready"), sem("exp_done"), sem("probs_ready"))
        aT_done, aT_masked = sem("aT_done"), sem("aT_masked")
        pT_done, pT_copied, pv_done = sem("pT_done"), sem("pT_copied"), sem("pv_done")
        mix_hi_ready, mix_lo_ready = sem("mix_hi_ready"), sem("mix_lo_ready")
        ds_done, states_ready = sem("ds_done"), sem("states_ready")
        gg_nabs, gg_log, gg_logsig, gg_sig, gla_gate = sem("gg_nabs"), sem("gg_log"), sem("gg_logsig"), sem("gg_sig"), sem("gla_gate")
        o_done, o_sq, o_ms, o_rough, o_ready, oT_done = (
            sem("o_done"), sem("o_sq"), sem("o_ms"), sem("o_rough"), sem("o_ready"), sem("oT_done"))
        pp0_copied, pp1_copied, e_ready = sem("pp0_copied"), sem("pp1_copied"), sem("e_ready")
        h_ready = sem("h_ready")
        relu_done, squared, hidT_done, hid_hi, hid_lo = (
            sem("relu_done"), sem("squared"), sem("hidT_done"), sem("hid_hi"), sem("hid_lo"))
        gate_done, out_ready, stored = sem("gate_done"), sem("out_ready"), sem("stored")
        dve_chain, act_chain, pool_chain = sem("dve_chain"), sem("act_chain"), sem("pool_chain")

        def cols_chunk(w, k0, n0):
            return w[k0 * P:(k0 + 4) * P, bass.ds(n0, NW)].rearrange("(k p) n -> p k n", p=P)

        def rows_chunk(w, r0):
            return w[bass.ds(r0, 2 * P), :].rearrange("(k p) n -> p k n", p=P)

        def raw_slot(c, k):
            return w_raw[:, c % RAW, :].rearrange("p (k n) -> p k n", k=k)

        def halfmat(buf, v, k):
            return buf[:, v % PAIRS, :].rearrange("p (k n) -> p k n", k=k)

        block = ctx.enter_context(nc.Block())

        @block.sync
        def _(sp):
            def load(c, src, k):
                if c >= RAW:
                    sp.wait_ge(lo_done, 2 * (c - RAW) + 2)
                nc.sync.dma_start(raw_slot(c, k), src).then_inc(raw_ready[c % RAW], 16)

            for t in range(T):
                nc.sync.dma_start(h[:, t, :], x[t * P:(t + 1) * P, :]).then_inc(x_in, 16)
            c = 0
            for i, n0 in enumerate(GROUP_COLS):
                if i == 5:
                    sp.wait_ge(lo_done, 2 * (c - RAW) + 2)
                    for n in range(2):
                        nc.sync.dma_start(raw_slot(c, 4)[:, 2 * n:2 * n + 2, :],
                                          w_pp[:, n * NW:(n + 1) * NW].rearrange("(k p) n -> p k n", p=P)
                                          ).then_inc(raw_ready[c % RAW], 16)
                    c += 1
                for k0 in (0, 4):
                    load(c, cols_chunk(w_in, k0, n0), 4)
                    c += 1
            for k0 in range(0, KT, 2):
                load(c, rows_chunk(w_out, k0 * P), 2)
                c += 1
            for k0 in (0, 4):
                load(c, cols_chunk(w_up, k0, 0), 4)
                c += 1
            with sp.Fori(1, GROUPS) as g:
                for j in range(4):
                    sp.wait_ge(lo_done, LOOP_HALVES * g + (2 * (c + j - RAW) + 2 - LOOP_HALVES))
                    if j < 2:
                        nc.sync.dma_start(raw_slot(c + j, 4), cols_chunk(w_up, 4 * j, g * NW)
                                          ).then_inc(raw_ready[(c + j) % RAW], 16)
                    else:
                        nc.sync.dma_start(raw_slot(c + j, 2), rows_chunk(w_down, g * NW + ((j - 2) * 2 * P - NW))
                                          ).then_inc(raw_ready[(c + j) % RAW], 16)
            c += 4 * (GROUPS - 1)
            for j in range(2):
                load(c, rows_chunk(w_down, (GROUPS - 1) * NW + j * 2 * P), 2)
                c += 1
            for n0 in (0, NW):
                for k0 in (0, 4):
                    load(c, cols_chunk(w_gate, k0, n0), 4)
                    c += 1
            for i in range(4):
                n, t = i // 2, i % 2
                sp.wait_ge(out_ready, i + 1)
                nc.sync.dma_start(out[t * P:(t + 1) * P, n * NW:(n + 1) * NW],
                                  gate_tmp[:, n, t, :]).then_inc(stored, 16)
            sp.wait_ge(stored, 16 * 4)

        def raw_value(c):
            return 16 * (c // RAW + 1) + (16 if c >= H_PP // 2 and c % RAW == H_PP // 2 % RAW else 0)

        @block.scalar
        def _(act):
            def split(v):
                if v >= PAIRS:
                    act.wait_ge(half_used, v - PAIRS + 1)
                act.wait_ge(raw_ready[(v // 2) % RAW], raw_value(v // 2))
                nc.scalar.activation(w_hi[:, v % PAIRS, :],
                                     w_raw[:, (v // 2) % RAW, (v % 2) * HALF:(v % 2 + 1) * HALF],
                                     ACT.Copy).then_inc(hi_done, 1)

            links = [0]

            def link(ins):
                links[0] += 1
                ins.then_inc(act_chain, 1)
                act.wait_ge(act_chain, links[0])

            def rough_rsqrt(dst, src, s):
                link(nc.scalar.activation(dst, src, ACT.Ln))
                nc.scalar.activation(dst, dst, ACT.Exp, scale=-0.5).then_inc(s, 1)

            def group_out(i):
                act.wait_ge(half_used, H_GROUP[i] + 4)
                if i == 0:
                    act.wait_ge(rs_ready, 1)
                for t in range(T):
                    last = nc.scalar.activation(z[:, i, t, :], ps[:, 2 * (i % 2) + t, :], ACT.Copy, scale=rs[:, t:t + 1])
                last.then_inc(z_ready, 1)

            nc.scalar.dma_start(gain_rows[0:8, :], g_mix.rearrange("(k p) -> k p", p=P)).then_inc(rows_in, 16)
            nc.scalar.dma_start(gain_rows[8:16, :], g_ffn.rearrange("(k p) -> k p", p=P)).then_inc(rows_in, 16)
            nc.scalar.dma_start(gain_rows[16:24, :], g_gate.rearrange("(k p) -> k p", p=P)).then_inc(rows_in, 16)
            nc.scalar.dma_start(w_ga[:, :, :], w_in[:, C_GA:C_GA + LOWRANK].rearrange("(k p) n -> p k n", p=P)).then_inc(ga_in, 16)
            nc.scalar.preload_act_table(ACT.Sin)
            act.wait_ge(trig_arg, 1)
            nc.scalar.activation(sin_t[:, :], angle[:, :], ACT.Sin).then_inc(trig_ready, 1)
            nc.scalar.activation(cos_t[:, :], turns[:, :], ACT.Sin).then_inc(trig_ready, 1)
            nc.scalar.preload_act_table_set("natural_log_exp_and_others")
            act.wait_ge(x_in, 16 * T)
            for t in range(T):
                nc.scalar.activation(scratch[:, t * D:(t + 1) * D], h[:, t, :], ACT.Square,
                                     accum_out=ss[:, t:t + 1]).then_inc(ss_ready, 1)
            for b in range(4):
                act.wait_ge(xg_ready, b + 1)
                nc.scalar.activation(act_hi[:, 2 * b:2 * b + 2, :], act3[:, 2 * b:2 * b + 2, :],
                                     ACT.Copy).then_inc(act_hi_ready, 1)
                if b == 1:
                    for v in (0, 1):
                        split(v)
            for v in (2, 3):
                split(v)
            act.wait_ge(ms_ready, 1)
            rough_rsqrt(rs[:, 0:T], ms[:, 0:T], rough_ready)
            act.wait_ge(p_T, 1)
            nc.scalar.activation(p_hi[:, :, :], ps[:, 2, :].rearrange("p (k s) -> p k s", k=2), ACT.Copy).then_inc(p_hi_ready, 1)
            act.wait_ge(ga_done, 1)
            nc.scalar.activation(ga_T[:, :], ps[0:LOWRANK, 4, 0:SEQ], ACT.Copy).then_inc(ga_copied, 1)
            split(4)
            split(5)
            act.wait_ge(neg_abs_ready, 1)
            link(nc.scalar.activation(la_nabs[:, :, :], la_nabs[:, :, :], ACT.Exp))
            nc.scalar.activation(la_nabs[:, :, :], la_nabs[:, :, :], ACT.Ln, bias=one[:, 0:1]).then_inc(log1p_ready, 1)
            split(6)
            split(7)
            group_out(0)
            act.wait_ge(z_ready, 1)
            nc.scalar.activation(squares, z[:, Z_MQ, :, :].rearrange("p t n -> p (t n)"), ACT.Square).then_inc(sq_ready, 1)
            split(8)
            act.wait_ge(cums_done, 1)
            nc.scalar.activation(dec[:, :, :, :].rearrange("p t b n -> p t (b n)"), ps[:, 6:8, :], ACT.Exp).then_inc(decays_ready, 1)
            nc.scalar.activation(inv_dec[:, :, :], ps[:, 6:8, 0:256], ACT.Exp, scale=-1.0).then_inc(decays_ready, 1)
            nc.scalar.activation(decay[:, :, :, :].rearrange("p a t c -> p (a t c)"), ps[:, 4, 0:8], ACT.Exp).then_inc(decays_ready, 1)
            split(9)
            act.wait_ge(msq_ready, 1)
            rough_rsqrt(rs_q[:, :], ss_q[:, :], rough_qk)
            split(10)
            split(11)
            group_out(1)
            act.wait_ge(z_ready, 2)
            act.wait_ge(msq_ready, 1)
            nc.scalar.activation(squares, z[:, Z_MK, :, :].rearrange("p t n -> p (t n)"), ACT.Square).then_inc(sq_ready, 1)
            split(12)
            act.wait_ge(qkT_done, 1)
            nc.scalar.activation(q_T.rearrange("p (a h) s -> p a (h s)", a=2), ps[:, 4:6, :], ACT.Copy).then_inc(qkT_copied, 1)
            split(13)
            act.wait_ge(msq_ready, 2)
            rough_rsqrt(rs_k[:, :], ss_k[:, :], rough_qk)
            split(14)
            split(15)
            group_out(2)
            split(16)
            act.wait_ge(qkT_done, 2)
            nc.scalar.activation(k_T.rearrange("p (a h) s -> p a (h s)", a=2), ps[:, 6:8, :], ACT.Copy).then_inc(qkT_copied, 1)
            split(17)
            act.wait_ge(glaT_done, 1)
            nc.scalar.activation(qd_T[:, :, :, :].rearrange("p a t c -> p (a t c)"), ps[:, 4, :], ACT.Copy).then_inc(glaT_copied, 1)
            nc.scalar.activation(ki_T[:, :, :, :].rearrange("p a t c -> p (a t c)"), ps[:, 5, :], ACT.Copy).then_inc(glaT_copied, 1)
            split(18)
            split(19)
            group_out(3)
            split(20)

            def softmax_exp(i):
                act.wait_ge(bias_ready, i + 1)
                for hd in (2 * i, 2 * i + 1):
                    for t in range(T):
                        c = 2 * hd + t
                        s = slice(0, P) if t == 0 else slice(P, 3 * P)
                        nc.scalar.activation(probs[:, hd, s], probs[:, hd, s], ACT.Exp, scale=rs_q[:, c:c + 1],
                                             bias=nbias[:, c:c + 1], accum_out=rowsum[:, c:c + 1]).then_inc(exp_done, 1)

            softmax_exp(0)
            split(21)
            softmax_exp(1)
            split(22)
            act.wait_ge(gg_nabs, 1)
            link(nc.scalar.activation(silu_nabs, silu_nabs, ACT.Exp))
            nc.scalar.activation(silu_log, silu_nabs, ACT.Ln, bias=one[:, 0:1]).then_inc(gg_log, 1)
            split(23)
            group_out(4)
            split(24)
            act.wait_ge(half_used, H_PP + 1)
            nc.scalar.activation(e[:, :, 0:NW], ps[:, 2:4, :], ACT.Copy).then_inc(pp0_copied, 1)
            act.wait_ge(gg_logsig, 1)
            nc.scalar.activation(silu_nabs, silu_log, ACT.Exp).then_inc(gg_sig, 1)
            split(25)
            act.wait_ge(o_done, 1)
            nc.scalar.activation(o_squares.rearrange("p (b n) -> p b n", b=2), ps[:, 4:6, :], ACT.Square).then_inc(o_sq, 1)
            split(26)
            act.wait_ge(o_ms, 1)
            rough_rsqrt(rs_o[:, :], ss_o[:, :], o_rough)
            act.wait_ge(pT_done, 1)
            nc.scalar.activation(probs_T[:, 0:2, :], ps[:, 6:8, 0:384], ACT.Copy).then_inc(pT_copied, 1)
            split(27)
            act.wait_ge(pT_done, 2)
            nc.scalar.activation(probs_T[:, 2:4, :], ps[:, 6:8, 0:384], ACT.Copy).then_inc(pT_copied, 1)
            split(28)
            act.wait_ge(oT_done, 1)
            for b in range(2):
                nc.scalar.activation(mix_hi[:, 2 * b:2 * b + 2, :], ps[:, 4 + b, :].rearrange("p (k s) -> p k s", k=2),
                                     ACT.Copy).then_inc(mix_hi_ready, 1)
            split(29)
            group_out(5)
            split(30)
            act.wait_ge(pv_done, 1)
            for b in range(2):
                nc.scalar.activation(mix_hi[:, 4 + 2 * b:6 + 2 * b, :], ps[:, 6 + b, :].rearrange("p (k s) -> p k s", k=2),
                                     ACT.Copy).then_inc(mix_hi_ready, 1)
            split(31)
            act.wait_ge(pp1_copied, 1)
            act.wait_ge(gla_gate, T)
            for t in range(T):
                nc.scalar.activation(scratch[:, t * D:(t + 1) * D], e[:, t, :], ACT.Square,
                                     accum_out=ss[:, 6 + t:7 + t]).then_inc(ss_ready, 1)
            act.wait_ge(ms_ready, 2)
            rough_rsqrt(rs[:, 6:8], ms[:, 6:8], rough_ready)
            split(32)
            split(33)

            def residual(i, v):
                for v4 in range(v, v + 3):
                    split(v4)
                for b in range(4):
                    act.wait_ge(xg_ready, 4 * i + b + 1)
                    nc.scalar.activation(act_hi[:, 2 * b:2 * b + 2, :], act3[:, 2 * b:2 * b + 2, :],
                                         ACT.Copy).then_inc(act_hi_ready, 1)
                split(v + 3)
                for t in range(T):
                    nc.scalar.activation(scratch[:, t * D:(t + 1) * D], h[:, t, :], ACT.Square,
                                         accum_out=ss[:, 2 * i + t:2 * i + t + 1]).then_inc(ss_ready, 1)
                act.wait_ge(ms_ready, i + 2)
                rough_rsqrt(rs[:, 2 * i:2 * i + T], ms[:, 2 * i:2 * i + T], rough_ready)

            def relu_out(need):
                act.wait_ge(half_used, need)
                for t in range(T):
                    last = nc.scalar.activation(hidden[:, t, :], ps[:, t, :], ACT.Relu, scale=rs[:, 2 + t:3 + t])
                last.then_inc(relu_done, 1)

            residual(1, H_UP0)
            act.wait_ge(rs_ready, 3)
            relu_out(H_LOOP)
            with act.Fori(1, GROUPS) as g:
                for j in range(LOOP_HALVES):
                    v = H_LOOP + j
                    act.wait_ge(half_used, LOOP_HALVES * g + (v - PAIRS + 1 - LOOP_HALVES))
                    act.wait_ge(raw_ready[(v // 2) % RAW], 16 * g + (raw_value(v // 2) - 16))
                    nc.scalar.activation(w_hi[:, v % PAIRS, :],
                                         w_raw[:, (v // 2) % RAW, (v % 2) * HALF:(v % 2 + 1) * HALF],
                                         ACT.Copy).then_inc(hi_done, 1)
                    if j == 3:
                        for b in range(2):
                            act.wait_ge(hidT_done, 2 * g + (b - 1))
                            nc.scalar.activation(mix_hi[:, 2 * b:2 * b + 2, :], ps[:, 2 + b, :].rearrange("p (k s) -> p k s", k=2),
                                                 ACT.Copy).then_inc(hid_hi, 1)
                relu_out(LOOP_HALVES * g + (H_LOOP + 4 - LOOP_HALVES))
            for v in range(H_DOWN_LAST, H_DOWN_LAST + 4):
                split(v)
            for b in range(2):
                act.wait_ge(hidT_done, 2 * GROUPS + b - 1)
                nc.scalar.activation(mix_hi[:, 2 * b:2 * b + 2, :], ps[:, 2 + b, :].rearrange("p (k s) -> p k s", k=2),
                                     ACT.Copy).then_inc(hid_hi, 1)
            residual(2, H_GATE)
            for v in range(H_GATE + 4, H_END):
                split(v)
            nc.scalar.preload_act_table(ACT.Sigmoid)
            act.wait_ge(rs_ready, 4)
            for n in range(2):
                act.wait_ge(half_used, H_GATE + 4 * n + 4)
                for t in range(T):
                    nc.scalar.activation(gate_tmp[:, n, t, :], ps[:, 4 + 2 * n + t, :], ACT.Sigmoid,
                                         scale=rs[:, 4 + t:5 + t]).then_inc(gate_done, 1)

        @block.vector
        def _(dve):
            links = [0]

            def link(ins):
                links[0] += 1
                ins.then_inc(dve_chain, 1)
                dve.wait_ge(dve_chain, links[0])

            def split(v):
                dve.wait_ge(hi_done, v + 1)
                nc.vector.tensor_tensor(w_lo[:, v % PAIRS, :],
                                        w_raw[:, (v // 2) % RAW, (v % 2) * HALF:(v % 2 + 1) * HALF],
                                        w_hi[:, v % PAIRS, :].bitcast(F32), ALU.subtract).then_inc(lo_done, 1)

            def refine(y, m, tmp):
                link(nc.vector.tensor_tensor(tmp, y, y, ALU.mult))
                link(nc.vector.tensor_tensor(tmp, tmp, m, ALU.mult))
                link(nc.vector.tensor_scalar(tmp, tmp, -0.5, 1.5, ALU.mult, ALU.add))
                return nc.vector.tensor_tensor(y, y, tmp, ALU.mult)

            def mean_eps(dst, src, width, s):
                nc.vector.tensor_scalar(dst, src, 1.0 / width, EPS, ALU.mult, ALU.add).then_inc(s, 1)

            nc.vector.memset(one[:, :], 1.0).then_inc(consts, 1)
            dve.wait_ge(pos_in, 16 * T)
            dve.wait_ge(bc_in, 16 * 5)
            link(nc.vector.tensor_copy(pos_f[:, :], pos_i[:, :]))
            for t in range(T):
                last = nc.vector.tensor_scalar(angle[:, t * 64:(t + 1) * 64], inv_b[:, :], pos_f[:, t:t + 1], None, ALU.mult)
            link(last)
            link(nc.vector.tensor_scalar(turns[:, :], angle[:, :], 1.0 / TWO_PI, ROUND, ALU.mult, ALU.add))
            link(nc.vector.tensor_scalar(turns[:, :], turns[:, :], -ROUND, None, ALU.add))
            for part in (PI_A, PI_B, PI_C):
                link(nc.vector.scalar_tensor_tensor(angle[:, :], turns[:, :], -part, angle[:, :], ALU.mult, ALU.add))
            link(nc.vector.tensor_scalar(angle[:, :], angle[:, :], PI_BELOW, -PI_BELOW, ALU.min, ALU.max))
            link(nc.vector.scalar_tensor_tensor(turns[:, :], angle[:, :], -1.0, angle[:, :], ALU.mult, ALU.min))
            nc.vector.tensor_scalar(turns[:, :], turns[:, :], HALF_PI, None, ALU.add).then_inc(trig_arg, 1)

            dve.wait_ge(gains_T, 1)
            nc.vector.tensor_copy(gains[:, :], ps[:, 3, 0:24]).then_inc(gains_ready, 1)
            dve.wait_ge(gains_ready, 1)

            def gain_transposed(i, b):
                dve.wait_ge(x_T, 4 * i + b + 1)
                nc.vector.tensor_tensor(act3[:, 2 * b:2 * b + 2, :], ps[:, T_BANK[i] + b, :].rearrange("p (k s) -> p k s", k=2),
                                        gains[:, 8 * i + 2 * b:8 * i + 2 * b + 2].unsqueeze(2).broadcast_to([P, 2, SEQ]),
                                        ALU.mult).then_inc(xg_ready, 1)

            def low_transposed(i, b):
                dve.wait_ge(act_hi_ready, 4 * i + b + 1)
                nc.vector.tensor_tensor(act_lo[:, 2 * b:2 * b + 2, :], act3[:, 2 * b:2 * b + 2, :],
                                        act_hi[:, 2 * b:2 * b + 2, :].bitcast(F32), ALU.subtract).then_inc(act_lo_ready, 1)

            for b in range(4):
                gain_transposed(0, b)
            low_transposed(0, 0)
            low_transposed(0, 1)
            split(0)
            split(1)
            low_transposed(0, 2)
            low_transposed(0, 3)
            split(2)
            split(3)
            dve.wait_ge(ss_ready, T)
            mean_eps(ms[:, 0:T], ss[:, 0:T], D, ms_ready)
            dve.wait_ge(p_hi_ready, 1)
            nc.vector.tensor_tensor(p_lo[:, :, :], ps[:, 2, :].rearrange("p (k s) -> p k s", k=2), p_hi[:, :, :].bitcast(F32),
                                    ALU.subtract).then_inc(p_lo_ready, 1)
            dve.wait_ge(rough_ready, 1)
            refine(rs[:, 0:T], ms[:, 0:T], nt[:, 0:T]).then_inc(rs_ready, 1)
            split(4)
            split(5)
            dve.wait_ge(rs_ready, 1)
            dve.wait_ge(apre_done, 1)
            for t in range(T):
                last = nc.vector.scalar_tensor_tensor(la[:, t, :], ps[:, 5, t * 256:(t + 1) * 256], rs[:, t:t + 1], b_a_b[:, :],
                                                      ALU.mult, ALU.add)
            link(last)
            nc.vector.scalar_tensor_tensor(la_nabs[:, :, :], la[:, :, :], -1.0, la[:, :, :], ALU.mult, ALU.min).then_inc(neg_abs_ready, 1)
            dve.wait_ge(log1p_ready, 1)
            nc.vector.scalar_tensor_tensor(la[:, :, :], la[:, :, :], 0.0, la_nabs[:, :, :], ALU.min, ALU.subtract).then_inc(la_ready, 1)
            split(6)
            split(7)

            def mean_square(i, ssd):
                dve.wait_ge(sq_ready, i + 1)
                link(nc.vector.tensor_reduce(ssd[:, :].rearrange("p (h t) -> p t h", h=HEADS),
                                             squares.rearrange("p (t h d) -> p t h d", t=T, h=HEADS), AXIS_X, ALU.add))
                mean_eps(ssd[:, :], ssd[:, :], HD, msq_ready)

            def rope_low(i, tab):
                zz = z[:, Z_MQ + i, :, :].rearrange("p t (h d) -> p t h d", h=HEADS)
                x1, x2 = zz[:, :, :, 0:64], zz[:, :, :, 64:128]
                if i:
                    dve.wait_ge(qk_ready, 2 * i)
                bc = lambda j: tab[:, j, :, :].unsqueeze(2).broadcast_to([P, T, HEADS, 64])
                nc.vector.tensor_tensor(rope_tmp[:, 0], x1, bc(0), ALU.mult)
                link(nc.vector.tensor_tensor(rope_tmp[:, 1], x2, bc(1), ALU.mult))
                dve.wait_ge(rope_high, 2 * (i + 1))
                nc.vector.tensor_tensor(x1, rope_tmp[:, 0], rope_tmp[:, 1], ALU.subtract).then_inc(qk_ready, 1)
                nc.vector.tensor_tensor(x2, rope_tmp[:, 2], rope_tmp[:, 3], ALU.add).then_inc(qk_ready, 1)

            mean_square(0, ss_q)
            split(8)
            dve.wait_ge(tables_ready, 1)
            rope_low(0, rope_q)
            split(9)
            dve.wait_ge(rough_qk, 1)
            link(refine(rs_q[:, :], ss_q[:, :], nq[:, :]))
            link(nc.vector.tensor_scalar(rs_q[:, :], rs_q[:, :], HD ** -0.5, None, ALU.mult))
            split(10)
            split(11)
            mean_square(1, ss_k)
            split(12)
            rope_low(1, rope_k)
            split(13)
            dve.wait_ge(rough_qk, 2)
            link(refine(rs_k[:, :], ss_k[:, :], nq[:, :]))
            dve.wait_ge(qk_ready, 4)
            for t in range(T):
                kk = z[:, Z_MK, t, :].rearrange("p (h d) -> p h d", h=HEADS)
                nc.vector.tensor_tensor(kk, kk, rs_k[:, t:8:2].unsqueeze(2).broadcast_to([P, HEADS, HD]), ALU.mult).then_inc(qk_ready, 1)
            split(14)
            split(15)
            split(16)
            dve.wait_ge(z_ready, 3)
            dve.wait_ge(decays_ready, 3)
            gq, gk = z[:, Z_GQK, :, 0:256], z[:, Z_GQK, :, 256:512]
            nc.vector.scalar_tensor_tensor(dec[:, :, 0, :], gq, DK ** -0.5, dec[:, :, 0, :], ALU.mult, ALU.mult).then_inc(gla_ops, 1)
            nc.vector.tensor_tensor(inv_dec[:, :, :], gk, inv_dec[:, :, :], ALU.mult).then_inc(gla_ops, 1)
            nc.vector.tensor_tensor(dec[:, :, 1, :], gk, dec[:, :, 1, :], ALU.mult).then_inc(gla_ops, 1)
            split(17)
            split(18)
            split(19)

            def mask_scores(hd):
                dve.wait_ge(scores_done, hd + 1)
                b = 4 + (hd + 2) % 4
                for t in range(T):
                    lo_c, hi_c = (0, P) if t == 0 else (P, 3 * P)
                    nc.vector.tensor_tensor_reduce(
                        out=probs[:, hd, lo_c:hi_c], in0=ps[:, b, lo_c:hi_c], in1=causal[:, P if t == 0 else 0:2 * P],
                        scale=1.0, scalar=-3e38, op0=ALU.add, op1=ALU.max,
                        accum_out=qmax[:, 2 * hd + t:2 * hd + t + 1]).then_inc(masked, 1)

            def softmax_bias(i):
                c = slice(4 * i, 4 * i + 4)
                dve.wait_ge(masked, 4 * (i + 1))
                nc.vector.scalar_tensor_tensor(nbias[:, c], qmax[:, c], -1.0, rs_q[:, c], ALU.mult, ALU.mult).then_inc(bias_ready, 1)

            def normalise(i):
                c = slice(4 * i, 4 * i + 4)
                dve.wait_ge(exp_done, 4 * (i + 1))
                link(nc.vector.reciprocal(rinv[:, c], rowsum[:, c]))
                for hd in (2 * i, 2 * i + 1):
                    for t in range(T):
                        lo_c, hi_c = (0, P) if t == 0 else (P, 3 * P)
                        last = nc.vector.tensor_scalar(probs[:, hd, lo_c:hi_c], probs[:, hd, lo_c:hi_c],
                                                       rinv[:, 2 * hd + t:2 * hd + t + 1], None, ALU.mult)
                last.then_inc(probs_ready, 1)

            mask_scores(0)
            mask_scores(1)
            softmax_bias(0)
            split(20)
            mask_scores(2)
            mask_scores(3)
            softmax_bias(1)
            split(21)
            dve.wait_ge(aT_done, 2)
            dve.wait_ge(consts, 3)
            for b in range(2):
                nc.vector.copy_predicated(a_T[:, b, :, :, :].rearrange("p t a c -> p (t a) c"),
                                          tri[:, :].bitcast(I32).unsqueeze(1).broadcast_to([P, 4, P]),
                                          ps[:, 6 + b, :].rearrange("p (m c) -> p m c", m=4)).then_inc(aT_masked, 1)
            dve.wait_ge(z_ready, 4)
            gg = z[:, Z_GG, :, :].rearrange("p t n -> p (t n)")
            nc.vector.scalar_tensor_tensor(silu_nabs, gg, -1.0, gg, ALU.mult, ALU.min).then_inc(gg_nabs, 1)
            split(22)
            normalise(0)
            split(23)
            dve.wait_ge(gg_log, 1)
            nc.vector.scalar_tensor_tensor(silu_log, gg, 0.0, silu_log, ALU.min, ALU.subtract).then_inc(gg_logsig, 1)
            normalise(1)
            split(24)
            dve.wait_ge(ds_done, 1)
            link(nc.vector.tensor_copy(state[:, 0, :, :], ps[:, 6, 0:256].rearrange("p (a v) -> p a v", a=2)))
            for n, bank, c0 in ((1, 7, 0), (2, 6, 256)):
                for a in range(2):
                    last = nc.vector.scalar_tensor_tensor(
                        state[:, n, a, :], state[:, n - 1, a, :], decay[:, a, n // 2, n % 2:n % 2 + 1],
                        ps[:, bank, c0 + a * DV:c0 + (a + 1) * DV], ALU.mult, ALU.add)
                if n == 1:
                    link(last)
            last.then_inc(states_ready, 1)
            split(25)
            dve.wait_ge(half_used, H_PP + 2)
            nc.vector.tensor_copy(e[:, :, NW:D], ps[:, 0:2, :]).then_inc(pp1_copied, 1)
            dve.wait_ge(o_sq, 1)
            link(nc.vector.tensor_reduce(ss_o[:, :], o_squares.rearrange("p (m d) -> p m d", d=DV), AXIS_X, ALU.add))
            mean_eps(ss_o[:, :], ss_o[:, :], DV, o_ms)
            split(26)
            dve.wait_ge(o_rough, 1)
            link(refine(rs_o[:, :], ss_o[:, :], nq[:, :]))
            dve.wait_ge(gla_gate, T)
            for par in range(2):
                ov = o_gla.rearrange("p t (a r v) -> p t a r v", a=2, r=2)[:, :, :, par, :]
                gv_ = z[:, Z_GG, :, :].rearrange("p t (a r v) -> p t a r v", a=2, r=2)[:, :, :, par, :]
                link(nc.vector.tensor_tensor(
                    ov, ps[:, 4 + par, :].rearrange("p (t a v) -> p t a v", t=T, a=2),
                    rs_o[:, 4 * par:4 * par + 4].rearrange("p (t a) -> p t a", t=T).unsqueeze(3).broadcast_to([P, T, 2, DV]), ALU.mult))
                nc.vector.tensor_tensor(ov, ov, gv_, ALU.mult).then_inc(o_ready, 1)
            split(27)
            split(28)

            def mix_low(b):
                dve.wait_ge(mix_hi_ready, b + 1)
                nc.vector.tensor_tensor(mix_lo[:, 2 * b:2 * b + 2, :], ps[:, 4 + b, :].rearrange("p (k s) -> p k s", k=2),
                                        mix_hi[:, 2 * b:2 * b + 2, :].bitcast(F32), ALU.subtract).then_inc(mix_lo_ready, 1)

            mix_low(0)
            mix_low(1)
            split(29)
            split(30)
            mix_low(2)
            mix_low(3)
            split(31)
            dve.wait_ge(ss_ready, 2 * T)
            mean_eps(ms[:, 6:8], ss[:, 6:8], D, ms_ready)
            split(32)
            dve.wait_ge(rough_ready, 2)
            refine(rs[:, 6:8], ms[:, 6:8], nt[:, 6:8]).then_inc(rs_ready, 1)
            dve.wait_ge(rs_ready, 2)
            dve.wait_ge(ple_in, 16)
            for t in range(T):
                last = nc.vector.scalar_tensor_tensor(e[:, t, :], e[:, t, :], rs[:, 6 + t:7 + t], g_ple_b[:, :], ALU.mult, ALU.mult)
            last.then_inc(e_ready, 1)
            split(33)

            def residual(i, v, need, bank):
                for v4 in range(v, v + 3):
                    split(v4)
                dve.wait_ge(half_used, need)
                for n in range(2):
                    for t in range(T):
                        nc.vector.tensor_tensor(h[:, t, n * NW:(n + 1) * NW], ps[:, bank(t, n), :],
                                                h[:, t, n * NW:(n + 1) * NW], ALU.add).then_inc(h_ready, 1)
                for b in range(4):
                    gain_transposed(i, b)
                    if b:
                        low_transposed(i, b - 1)
                low_transposed(i, 3)
                split(v + 3)
                dve.wait_ge(ss_ready, T * (i + 2))
                mean_eps(ms[:, 2 * i:2 * i + T], ss[:, 2 * i:2 * i + T], D, ms_ready)
                dve.wait_ge(rough_ready, i + 2)
                refine(rs[:, 2 * i:2 * i + T], ms[:, 2 * i:2 * i + T], nt[:, 2 * i:2 * i + T]).then_inc(rs_ready, 1)

            residual(1, H_UP0, H_OUT + KT, lambda t, n: 2 * t + n)
            dve.wait_ge(relu_done, 1)
            nc.vector.tensor_tensor(hidden, hidden, hidden, ALU.mult).then_inc(squared, 1)
            with dve.Fori(1, GROUPS) as g:
                for j in range(LOOP_HALVES):
                    v = H_LOOP + j
                    dve.wait_ge(hi_done, LOOP_HALVES * g + (v + 1 - LOOP_HALVES))
                    nc.vector.tensor_tensor(w_lo[:, v % PAIRS, :],
                                            w_raw[:, (v // 2) % RAW, (v % 2) * HALF:(v % 2 + 1) * HALF],
                                            w_hi[:, v % PAIRS, :].bitcast(F32), ALU.subtract).then_inc(lo_done, 1)
                    if j == 3:
                        for b in range(2):
                            dve.wait_ge(hid_hi, 2 * g + (b - 1))
                            nc.vector.tensor_tensor(mix_lo[:, 2 * b:2 * b + 2, :], ps[:, 2 + b, :].rearrange("p (k s) -> p k s", k=2),
                                                    mix_hi[:, 2 * b:2 * b + 2, :].bitcast(F32), ALU.subtract).then_inc(hid_lo, 1)
                dve.wait_ge(relu_done, g + 1)
                nc.vector.tensor_tensor(hidden, hidden, hidden, ALU.mult).then_inc(squared, 1)
            for v in range(H_DOWN_LAST, H_DOWN_LAST + 4):
                split(v)
            for b in range(2):
                dve.wait_ge(hid_hi, 2 * GROUPS + b - 1)
                nc.vector.tensor_tensor(mix_lo[:, 2 * b:2 * b + 2, :], ps[:, 2 + b, :].rearrange("p (k s) -> p k s", k=2),
                                        mix_hi[:, 2 * b:2 * b + 2, :].bitcast(F32), ALU.subtract).then_inc(hid_lo, 1)
            residual(2, H_GATE, H_GATE, lambda t, n: 4 + 2 * t + n)
            for v in range(H_GATE + 4, H_END):
                split(v)
            dve.wait_ge(e_ready, 1)
            for i in range(4):
                n, t = i // 2, i % 2
                dve.wait_ge(gate_done, i + 1)
                gt = gate_tmp[:, n, t, :]
                link(nc.vector.tensor_tensor(gt, gt, e[:, t, n * NW:(n + 1) * NW], ALU.mult))
                nc.vector.tensor_tensor(gt, gt, h[:, t, n * NW:(n + 1) * NW], ALU.add).then_inc(out_ready, 1)

        @block.gpsimd
        def _(pool):
            links = [0]

            def link(ins):
                links[0] += 1
                ins.then_inc(pool_chain, 1)
                pool.wait_ge(pool_chain, links[0])

            for t in range(T):
                nc.gpsimd.dma_start(pos_i[:, t:t + 1], positions[t * P:(t + 1) * P].unsqueeze(1)).then_inc(pos_in, 16)
            nc.gpsimd.dma_start(inv_b[:, :], inv_freq.partition_broadcast(P)).then_inc(bc_in, 16)
            link(nc.gpsimd.memset(ident[:, :], 0.0))
            nc.gpsimd.affine_select(out=ident[:, :], in_=ident[:, :], compare_op=ALU.not_equal, fill=1.0, base=0,
                                    pattern=[[-1, P]], channel_multiplier=1).then_inc(consts, 1)
            nc.gpsimd.dma_start(b_a_b[:, :], b_a.partition_broadcast(P)).then_inc(bc_in, 16)
            nc.gpsimd.dma_start(g_gla_b[:, :], g_gla.partition_broadcast(P)).then_inc(bc_in, 16)
            nc.gpsimd.dma_start(g_mq_b[:, :], g_mq.partition_broadcast(P)).then_inc(bc_in, 16)
            nc.gpsimd.dma_start(g_mk_b[:, :], g_mk.partition_broadcast(P)).then_inc(bc_in, 16)
            nc.gpsimd.dma_start(a2[:, :], w_a2).then_inc(a2_in, 16)
            for t in range(T):
                nc.gpsimd.dma_start(p_sb[:, t, :], p[t * P:(t + 1) * P, :]).then_inc(p_in, 16)
            nc.gpsimd.memset(tri[:, :], 1.0 / TAU).then_inc(pool_chain, 1)
            nc.gpsimd.memset(chunk_sum[:, :], 0.0).then_inc(pool_chain, 1)
            nc.gpsimd.memset(causal[:, :], 0.0).then_inc(pool_chain, 1)
            nc.gpsimd.memset(a_T[:, :, :, :, :], 0.0).then_inc(pool_chain, 1)
            links[0] += 4
            link(nc.gpsimd.memset(rest[:, :], 1.0 / TAU))
            nc.gpsimd.affine_select(out=tri[:, :], in_=tri[:, :], compare_op=ALU.is_ge, fill=0.0, base=0,
                                    pattern=[[1, P]], channel_multiplier=-1).then_inc(pool_chain, 1)
            nc.gpsimd.affine_select(out=causal[:, P:2 * P], in_=causal[:, P:2 * P], compare_op=ALU.is_ge, fill=MASKED, base=0,
                                    pattern=[[-1, P]], channel_multiplier=1).then_inc(pool_chain, 1)
            links[0] += 2
            link(nc.gpsimd.affine_select(out=rest[:, :], in_=rest[:, :], compare_op=ALU.is_gt, fill=0.0, base=0,
                                         pattern=[[-1, P]], channel_multiplier=1))
            link(nc.gpsimd.memset(tri[0:CHUNK, CHUNK:P], 0.0))
            link(nc.gpsimd.memset(rest[CHUNK:P, 0:CHUNK], 0.0))
            link(nc.gpsimd.memset(chunk_sum[0:CHUNK, 0:1], 1.0 / TAU))
            nc.gpsimd.memset(chunk_sum[CHUNK:P, 1:2], 1.0 / TAU).then_inc(consts, 1)
            nc.gpsimd.dma_start(g_ple_b[:, :], g_ple.partition_broadcast(P)).then_inc(ple_in, 16)
            pool.wait_ge(consts, 3)
            pool.wait_ge(trig_ready, 2)
            pool.wait_ge(bc_in, 16 * 5)
            for tab, gb in ((rope_q, g_mq_b), (rope_k, g_mk_b)):
                for j, (trig, g0) in enumerate(((cos_t, 0), (sin_t, 64), (cos_t, 64), (sin_t, 0))):
                    last = nc.gpsimd.tensor_tensor(tab[:, j, :, :], trig[:, :].rearrange("p (t d) -> p t d", t=T),
                                                   gb[:, g0:g0 + 64].unsqueeze(1).broadcast_to([P, T, 64]), ALU.mult)
            last.then_inc(tables_ready, 1)
            pool.wait_ge(tables_ready, 1)
            for i, tab in ((0, rope_q), (1, rope_k)):
                pool.wait_ge(z_ready, i + 1)
                zz = z[:, Z_MQ + i, :, :].rearrange("p t (h d) -> p t h d", h=HEADS)
                bc = lambda j: tab[:, j, :, :].unsqueeze(2).broadcast_to([P, T, HEADS, 64])
                if i:
                    pool.wait_ge(qk_ready, 2)
                nc.gpsimd.tensor_tensor(rope_tmp[:, 2], zz[:, :, :, 64:128], bc(2), ALU.mult).then_inc(rope_high, 1)
                nc.gpsimd.tensor_tensor(rope_tmp[:, 3], zz[:, :, :, 0:64], bc(3), ALU.mult).then_inc(rope_high, 1)
            pool.wait_ge(gg_sig, 1)
            gg = z[:, Z_GG, :, :].rearrange("p t n -> p (t n)")
            link(nc.gpsimd.tensor_tensor(gg, gg, silu_nabs, ALU.mult))
            for t in range(T):
                g3 = z[:, Z_GG, t, :].rearrange("p (h v) -> p h v", h=HEADS)
                nc.gpsimd.tensor_tensor(g3, g3, g_gla_b[:, :].unsqueeze(1).broadcast_to([P, HEADS, DV]), ALU.mult).then_inc(gla_gate, 1)

        @block.tensor
        def _(pe):
            def product(v, hi, lo, k0, kn, bank, first, last, cols, before_t1=None):
                wh, wl = halfmat(w_hi, v, kn), halfmat(w_lo, v, kn)
                order = [(k, [n]) for n in range(cols // NW) for k in range(kn)] if last and cols > NW else \
                    [(k, list(range(cols // NW))) for k in range(kn)]
                for k, ns in order:
                    for t in range(T):
                        if before_t1 and k == 0 and t == 1:
                            pe.wait_ge(*before_t1)
                        sh = hi[:, k0 + k, t * P:(t + 1) * P]
                        sl = lo[:, k0 + k, t * P:(t + 1) * P]
                        for n in ns:
                            w = slice(n * NW, (n + 1) * NW)
                            nc.tensor.matmul(ps[:, bank(t, n), :], sh, wh[:, k, w], start=first and k == 0, stop=False)
                            nc.tensor.matmul(ps[:, bank(t, n), :], sh, wl[:, k, w], start=False, stop=False)
                        for n in ns:
                            w = slice(n * NW, (n + 1) * NW)
                            mm = nc.tensor.matmul(ps[:, bank(t, n), :], sl, wh[:, k, w], start=False, stop=last and k == kn - 1)
                mm.then_inc(half_used, 1)

            def transposes(i, b):
                for k in range(2):
                    for t in range(T):
                        c = (k * T + t) * P
                        kt = 2 * b + k
                        mm = nc.tensor.transpose(ps[:, T_BANK[i] + b, c:c + P], h[:, t, kt * P:(kt + 1) * P], ident[:, :])
                mm.then_inc(x_T, 1)

            pe.wait_ge(rows_in, 16 * 3)
            pe.wait_ge(consts, 3)
            nc.tensor.transpose(ps[:, 3, 0:24], gain_rows[:, :], ident[0:24, 0:24]).then_inc(gains_T, 1)
            pe.wait_ge(x_in, 16 * T)
            for b in range(4):
                transposes(0, b)
            pe.wait_ge(p_in, 16 * T)
            for k in range(2):
                for t in range(T):
                    mm = nc.tensor.transpose(ps[:, 2, (k * T + t) * P:(k * T + t + 1) * P], p_sb[:, t, k * P:(k + 1) * P], ident[:, :])
            mm.then_inc(p_T, 1)
            pe.wait_ge(xg_ready, 4)
            pe.wait_ge(ga_in, 16)
            for k in range(KT):
                mm = nc.tensor.matmul(ps[0:LOWRANK, 4, 0:SEQ], w_ga[:, k, :], act3[:, k, :], start=k == 0, stop=k == KT - 1)
            mm.then_inc(ga_done, 1)

            def w_in_half(v):
                i = max(g for g in range(6) if H_GROUP[g] <= v)
                j = v - H_GROUP[i]
                if j == 0 and i >= 2:
                    pe.wait_ge(z_ready, i - 1)
                if j == 0 and i == 1:
                    pe.wait_ge(p_lo_ready, 1)
                    pe.wait_ge(gains_ready, 1)
                if j == 0 and i == 5:
                    pe.wait_ge(pp0_copied, 1)
                if i == 0:
                    pe.wait_ge(act_lo_ready, j + 1)
                pe.wait_ge(lo_done, v + 1)
                product(v, act_hi, act_lo, 2 * j, 2, lambda t, n: 2 * (i % 2) + t, j == 0, j == 3, NW)

            w_in_half(0)
            w_in_half(1)
            pe.wait_ge(ga_copied, 1)
            pe.wait_ge(a2_in, 16)
            for t in range(T):
                mm = nc.tensor.matmul(ps[:, 5, t * 256:(t + 1) * 256], ga_T[:, t * P:(t + 1) * P], a2[:, :], start=True, stop=True)
            mm.then_inc(apre_done, 1)
            for v in (2, 3, 4):
                w_in_half(v)
            pe.wait_ge(la_ready, 1)
            for t in range(T):
                nc.tensor.matmul(ps[:, 6 + t, 0:256], tri[:, :], la[:, t, :], start=True, stop=True)
                nc.tensor.matmul(ps[:, 6 + t, 256:512], rest[:, :], la[:, t, :], start=True, stop=True)
            for a in range(2):
                for t in range(T):
                    mm = nc.tensor.matmul(ps[:, 4, 4 * a + 2 * t:4 * a + 2 * t + 2], la[:, t, a * P:(a + 1) * P], chunk_sum[:, :],
                                          start=True, stop=True)
            mm.then_inc(cums_done, 1)
            for v in range(5, 9):
                w_in_half(v)

            def head_transposes(i, bank):
                for hd in range(HEADS):
                    for t in range(T):
                        c = ((hd % 2) * T + t) * P
                        mm = nc.tensor.transpose(ps[:, bank + hd // 2, c:c + P], z[:, Z_MQ + i, t, hd * HD:(hd + 1) * HD], ident[:, :])
                mm.then_inc(qkT_done, 1)

            pe.wait_ge(qk_ready, 2)
            pe.wait_ge(decays_ready, 3)
            head_transposes(0, 4)
            for v in range(9, 13):
                w_in_half(v)
            pe.wait_ge(qk_ready, 6)
            head_transposes(1, 6)
            w_in_half(13)
            pe.wait_ge(gla_ops, 2)
            pe.wait_ge(qkT_copied, 1)
            for a in range(2):
                for t in range(T):
                    c = (a * T + t) * P
                    nc.tensor.transpose(ps[:, 4, c:c + P], dec[:, t, 0, a * P:(a + 1) * P], ident[:, :])
                    mm = nc.tensor.transpose(ps[:, 5, c:c + P], inv_dec[:, t, a * P:(a + 1) * P], ident[:, :])
            mm.then_inc(glaT_done, 1)
            w_in_half(14)
            w_in_half(15)

            def scores(hd):
                b = 4 + (hd + 2) % 4
                nc.tensor.matmul(ps[:, b, 0:P], q_T[:, hd, 0:P], k_T[:, hd, 0:P], start=True, stop=True)
                nc.tensor.matmul(ps[:, b, P:3 * P], q_T[:, hd, P:2 * P], k_T[:, hd, :], start=True, stop=True).then_inc(scores_done, 1)

            pe.wait_ge(qkT_copied, 2)
            scores(0)
            scores(1)
            w_in_half(16)
            pe.wait_ge(glaT_copied, 2)
            scores(2)
            scores(3)
            w_in_half(17)
            pe.wait_ge(masked, 4)
            for par in range(2):
                r = slice(par * DK, (par + 1) * DK)
                for t in range(T):
                    for a in range(2):
                        c = (t * 2 + a) * P
                        mm = nc.tensor.matmul(ps[:, 6 + par, c:c + P], ki_T[r, a, t, :], qd_T[r, a, t, :], start=True, stop=True)
                mm.then_inc(aT_done, 1)
            w_in_half(18)
            w_in_half(19)

            def pp_half(n):
                pe.wait_ge(z_ready, 4 + n)
                pe.wait_ge(lo_done, H_PP + n + 1)
                product(H_PP + n, p_hi, p_lo, 0, 2, lambda t, _: 2 * (1 - n) + t, True, True, NW)

            pp_half(0)
            pe.wait_ge(z_ready, 5)
            pe.wait_ge(gla_ops, 3)
            pe.wait_ge(aT_masked, 2)
            for n in range(3):
                t, r = n // 2, slice((n % 2) * CHUNK, (n % 2 + 1) * CHUNK)
                bank, c0 = (7, 0) if n == 1 else (6, 256 * (n // 2))
                for hd in range(HEADS):
                    a, par = hd // 2, hd % 2
                    mm = nc.tensor.matmul(ps[par * DK:(par + 1) * DK, bank, c0 + a * DV:c0 + (a + 1) * DV],
                                          dec[r, t, 1, hd * DK:(hd + 1) * DK], z[r, Z_GV, t, hd * DV:(hd + 1) * DV],
                                          start=True, stop=True)
            mm.then_inc(ds_done, 1)
            pp_half(1)
            pe.wait_ge(states_ready, 1)
            pe.wait_ge(masked, 8)
            for par in range(2):
                r = slice(par * DK, (par + 1) * DK)
                for t in range(T):
                    for a in range(2):
                        hd = 2 * a + par
                        c = (t * 2 + a) * DV
                        nc.tensor.matmul(ps[:, 4 + par, c:c + DV], a_T[:, par, t, a, :], z[:, Z_GV, t, hd * DV:(hd + 1) * DV],
                                         start=True, stop=True)
                        for m in range(2):
                            n = 2 * t + m
                            if n:
                                mm = nc.tensor.matmul(ps[m * CHUNK:(m + 1) * CHUNK, 4 + par, c:c + DV],
                                                      qd_T[r, a, t, m * CHUNK:(m + 1) * CHUNK], state[r, n - 1, a, :],
                                                      start=False, stop=True, skip_group_check=True)
            mm.then_inc(o_done, 1)
            w_in_half(22)

            def prob_transposes(i):
                pe.wait_ge(probs_ready, i + 1)
                for hd in (2 * i, 2 * i + 1):
                    for m in range(3):
                        mm = nc.tensor.transpose(ps[:, 6 + hd % 2, m * P:(m + 1) * P], probs[:, hd, m * P:(m + 1) * P], ident[:, :])
                mm.then_inc(pT_done, 1)

            prob_transposes(0)
            w_in_half(23)
            pe.wait_ge(pT_copied, 1)
            prob_transposes(1)
            w_in_half(24)
            pe.wait_ge(o_ready, 2)
            for hd in range(HEADS):
                for t in range(T):
                    c = ((hd % 2) * T + t) * P
                    mm = nc.tensor.transpose(ps[:, 4 + hd // 2, c:c + P], o_gla[:, t, hd * DV:(hd + 1) * DV], ident[:, :])
            mm.then_inc(oT_done, 1)
            w_in_half(25)
            pe.wait_ge(pp1_copied, 1)

            def w_out_half(j, before_t1=None):
                if j in (0, 4):
                    pe.wait_ge(mix_lo_ready, 2 if j == 0 else 4)
                pe.wait_ge(lo_done, H_OUT + j + 1)
                product(H_OUT + j, mix_hi, mix_lo, j, 1, lambda t, n: 2 * t + n, j == 0, j == KT - 1, D, before_t1)

            w_out_half(0, (z_ready, 6))
            pe.wait_ge(pT_copied, 2)
            for hd in range(HEADS):
                d = slice(hd * HD, (hd + 1) * HD)
                c = (hd % 2) * SEQ
                nc.tensor.matmul(ps[:, 6 + hd // 2, c:c + SEQ], z[:, Z_MV, 0, d], probs_T[:, hd, 0:SEQ], start=True, stop=True)
                mm = nc.tensor.matmul(ps[:, 6 + hd // 2, c + P:c + SEQ], z[:, Z_MV, 1, d], probs_T[:, hd, SEQ:SEQ + P],
                                      start=False, stop=True, skip_group_check=True)
            mm.then_inc(pv_done, 1)
            for j in range(1, KT):
                w_out_half(j)

            def residual_transposes(i):
                for b in range(4):
                    if b % 2 == 0:
                        pe.wait_ge(h_ready, 4 * (i - 1) + 2 * (b // 2) + 2)
                    transposes(i, b)

            residual_transposes(1)
            for j in range(4):
                pe.wait_ge(act_lo_ready, 4 + j + 1)
                pe.wait_ge(lo_done, H_UP0 + j + 1)
                product(H_UP0 + j, act_hi, act_lo, 2 * j, 2, lambda t, n: t, j == 0, j == 3, NW)

            def hidden_transposes(g):
                pe.wait_ge(squared, g)
                for b in range(2):
                    for k in range(2):
                        for t in range(T):
                            kt = 2 * b + k
                            mm = nc.tensor.transpose(ps[:, 2 + b, (k * T + t) * P:(k * T + t + 1) * P],
                                                     hidden[:, t, kt * P:(kt + 1) * P], ident[:, :])
                    mm.then_inc(hidT_done, 1)

            def down(g, v0, lo_wait, first=False, last=False):
                for j in range(4):
                    if j % 2 == 0:
                        pe.wait_ge(hid_lo, 2 * g - 1 + j // 2)
                    pe.wait_ge(lo_done, lo_wait + j)
                    product(v0 + j, mix_hi, mix_lo, j, 1, lambda t, n: 4 + 2 * t + n, first and j == 0, last and j == 3, D)

            def ffn_group(g, first=False):
                hidden_transposes(g)
                for j in range(4):
                    pe.wait_ge(lo_done, LOOP_HALVES * g + (H_LOOP + j + 1 - LOOP_HALVES))
                    product(H_LOOP + j, act_hi, act_lo, 2 * j, 2, lambda t, n: t, j == 0, j == 3, NW)
                down(g, H_LOOP + 4, LOOP_HALVES * g + (H_LOOP + 5 - LOOP_HALVES), first)

            ffn_group(1, first=True)
            with pe.Fori(2, GROUPS) as g:
                ffn_group(g)
            hidden_transposes(GROUPS)
            down(GROUPS, H_DOWN_LAST, H_DOWN_LAST + 1, last=True)
            residual_transposes(2)
            for n in range(2):
                for j in range(4):
                    v = H_GATE + 4 * n + j
                    if n == 0:
                        pe.wait_ge(act_lo_ready, 8 + j + 1)
                    pe.wait_ge(lo_done, v + 1)
                    product(v, act_hi, act_lo, 2 * j, 2, lambda t, _: 4 + 2 * n + t, j == 0, j == 3, NW)


_INS = ["x", "p", "positions", "g_mix", "w_in", "w_gla_a2", "b_gla_a", "g_gla_out", "g_moba_q", "g_moba_k", "w_out",
        "g_ffn", "w_up", "w_down", "g_ple_gate", "w_ple_gate", "w_ple_proj", "g_ple_emb"]


def kernel(**inputs):
    import numpy as np
    import concourse.bacc as bacc
    from concourse.bass_utils import run_bass_kernel_spmd

    nc = bacc.Bacc("TRN2", target_bir_lowering=False, num_devices=1)
    arrays, args = {}, []

    def add(name, a):
        arrays[name] = a
        args.append(nc.dram_tensor(name, a.shape, mybir.dt.from_np(a.dtype), kind="ExternalInput").ap())

    for name in _INS:
        a = np.ascontiguousarray(inputs[name])
        while a.ndim > 1 and a.shape[0] == 1:
            a = a[0]
        add("in_" + name, a)
    half = HD // 2
    add("inv_freq", (np.float32(1.0) / np.float32(10000.0) ** (np.arange(half, dtype=np.float32) / np.float32(half))).astype(np.float32))
    args.append(nc.dram_tensor("out", (SEQ, D), F32, kind="ExternalOutput").ap())
    build(nc, *args)
    r = run_bass_kernel_spmd(nc, [arrays], core_ids=[0])
    return r.results[0]["out"].reshape(1, SEQ, D)
```

```python
import concourse.bass as bass
from concourse import mybir
from contextlib import ExitStack

F32 = mybir.dt.float32
F32R = mybir.dt.float32r
BF16 = mybir.dt.bfloat16
I32 = mybir.dt.int32
ACT = mybir.ActivationFunctionType
ALU = mybir.AluOpType
AXIS_X = mybir.AxisListType.X

P = 128
SEQ, D, D_FF, PLE = 256, 1024, 4096, 256
T = SEQ // P
KT = D // P
NW = 512
GROUPS = D_FF // NW
HEADS = 4
HD = 128
DK, DV = 64, 128
CHUNK = 64
LOWRANK = 16
TAU = 16.0
EPS = 1e-6
WARM_UP = 9
HALF = 1024
RAW, PAIRS = 8, 4
C_GQK, C_GV, C_GG, C_GA, C_MQ, C_MK, C_MV = 0, 512, 1024, 1536, 1552, 2064, 2576
GROUP_COLS = [C_MQ, C_MK, C_GQK, C_GG, C_GV, C_MV]
Z_MQ, Z_MK, Z_GQK, Z_GG, Z_GV, Z_MV = range(6)

H_PP = 4 * 5
H_GROUP = [0, 4, 8, 12, 16, H_PP + 2]
H_OUT = H_GROUP[5] + 4
H_UP0 = H_OUT + KT
H_LOOP = H_UP0 + 4
LOOP_HALVES = 8
H_DOWN_LAST = H_LOOP + LOOP_HALVES * (GROUPS - 1)
H_GATE = H_DOWN_LAST + 4
H_END = H_GATE + 8

TWO_PI = 6.283185307179586
PI_A = 6.28125
PI_B = 0.0019340515136719
PI_C = TWO_PI - PI_A - PI_B
ROUND = 12582912.0
HALF_PI = 1.5707963267948966
PI_BELOW = 3.1415925
MASKED = -1e30

GATE_PIECES = [(0, 0, 0, NW), (0, 1, 0, NW), (1, 0, 0, NW), (1, 1, 0, NW // 2), (1, 1, NW // 2, NW)]

T_BANK = [4, 4, 0]


def build(nc, x, p, positions, g_mix, w_in, w_a2, b_a, g_gla, g_mq, g_mk, w_out, g_ffn, w_up, w_down,
          g_gate, w_gate, w_pp, g_ple, inv_freq, out):
    ctx = ExitStack()
    with ctx:
        def sb(name, shape, dt=F32):
            return ctx.enter_context(nc.sbuf_tensor(name, shape, dt))

        def sem(name):
            return ctx.enter_context(nc.semaphore(name))

        w_raw = sb("w_raw", [P, RAW, HALF])
        w_hi = sb("w_hi", [P, PAIRS, HALF], F32R)
        w_lo = sb("w_lo", [P, PAIRS, HALF], F32R)
        act_hi = sb("act_hi", [P, KT, SEQ], F32R)
        act_lo = sb("act_lo", [P, KT, SEQ], F32R)
        mix_hi = sb("mix_hi", [P, KT, SEQ], F32R)
        mix_lo = sb("mix_lo", [P, KT, SEQ], F32R)
        work = sb("work", [P, HEADS * 384])
        h = sb("h", [P, T, D])
        z = sb("z", [P, 6, T, NW])
        qk_T = sb("qk_T", [P, 2 * HEADS * SEQ])
        g_ple_b = sb("g_ple_b", [P, D])
        scratch = sb("scratch", [P, 4 * T * 256])
        la = sb("la", [P, T, 256])
        la_nabs = sb("la_nabs", [P, T, 256])
        la_hi = sb("la_hi", [P, T, 256], F32R)
        la_lo = sb("la_lo", [P, T, 256], F32R)
        dec = sb("dec", [P, T, 2, 256])
        inv_dec = sb("inv_dec", [P, T, 256])
        qd_T = sb("qd_T", [P, 2, T, P])
        ki_T = sb("ki_T", [P, 2, T, P])
        a_T = sb("a_T", [P, 2, T, 2, P])
        state = sb("state", [P, 3, 2, DV])
        decay = sb("decay", [P, 2, T, 2])
        rope_q = sb("rope_q", [P, 4, T, 64])
        rope_k = sb("rope_k", [P, 4, T, 64])
        sin_t = sb("sin_t", [P, T * 64])
        cos_t = sb("cos_t", [P, T * 64])
        angle = sb("angle", [P, T * 64])
        turns = sb("turns", [P, T * 64])
        p_sb = sb("p_sb", [P, T, PLE])
        p_hi = sb("p_hi", [P, 2, SEQ], F32R)
        p_lo = sb("p_lo", [P, 2, SEQ], F32R)
        ident = sb("ident", [P, P])
        tri = sb("tri", [P, P])
        rest = sb("rest", [P, P])
        triangles = sb("triangles", [P, 2, P], F32R)
        chunk_sum = sb("chunk_sum", [P, 2])
        causal = sb("causal", [P, 2 * P])
        w_ga = sb("w_ga", [P, KT, LOWRANK])
        ga_pack = sb("ga_pack", [P, KT, P], F32R)
        ga_T = sb("ga_T", [2 * LOWRANK, SEQ])
        a2 = sb("a2", [2 * LOWRANK, 256])
        b_a_b = sb("b_a_b", [P, 256])
        g_gla_b = sb("g_gla_b", [P, DV])
        g_mq_b = sb("g_mq_b", [P, HD])
        g_mk_b = sb("g_mk_b", [P, HD])
        inv_b = sb("inv_b", [P, 64])
        pos_i = sb("pos_i", [P, T], I32)
        pos_f = sb("pos_f", [P, T])
        mix_rows = sb("mix_rows", [KT, P])
        gain_rows = sb("gain_rows", [2 * KT, P])
        gains = sb("gains", [P, 24])
        ss = sb("ss", [P, 8])
        rs = sb("rs", [P, 8])
        ms = sb("ms", [P, 8])
        nt = sb("nt", [P, 8])
        ss_q = sb("ss_q", [P, 8])
        rs_q = sb("rs_q", [P, 8])
        ss_k = sb("ss_k", [P, 8])
        rs_k = sb("rs_k", [P, 8])
        nq = sb("nq", [P, 8])
        qmax = sb("qmax", [P, 8])
        nbias = sb("nbias", [P, 8])
        rowsum = sb("rowsum", [P, 8])
        rinv = sb("rinv", [P, 8])
        ss_o = sb("ss_o", [P, 8])
        rs_o = sb("rs_o", [P, 8])
        one = sb("one", [P, 1])
        zeros = sb("zeros", [P, NW], BF16)
        ps = ctx.enter_context(nc.psum_tensor("ps", [P, 8, NW], F32))

        probs = work[:, :].rearrange("p (h c) -> p h c", h=HEADS)
        squares = work[:, 0:T * NW]
        q_T = qk_T[:, 0:HEADS * SEQ].rearrange("p (h s) -> p h s", h=HEADS)
        k_T = qk_T[:, HEADS * SEQ:].rearrange("p (h s) -> p h s", h=HEADS)
        e = qk_T[:, :].rearrange("p (t n) -> p t n", t=T)
        probs_T = z[:, Z_MQ:Z_MQ + 2, :, :].rearrange("p g t n -> p (g t n)")[:, 0:HEADS * 384].rearrange(
            "p (h c) -> p h c", h=HEADS)
        hidden = z[:, Z_MQ, :, :]
        o_gla = z[:, Z_GQK, :, :]
        gate_tmp = z[:, Z_MK:Z_MK + 2, :, :]
        rope_tmp = scratch[:, :].rearrange("p (i t h d) -> p i t h d", i=4, t=T, h=HEADS)
        o_squares = dec[:, :, :, :].rearrange("p t b n -> p (t b n)")
        silu_nabs = scratch[:, 0:T * NW]
        silu_log = scratch[:, T * NW:2 * T * NW]

        raw_ready = [sem(f"raw_ready{i}") for i in range(RAW)]
        hi_done, lo_done, half_used = sem("hi_done"), sem("lo_done"), sem("half_used")
        x_in = [sem(f"x_in{t}") for t in range(T)]
        ga_in, p_in, a2_in, mix_in, rows_in, pos_in, inv_in, b_in, bc_in, ple_in = (
            sem(n) for n in ("ga_in", "p_in", "a2_in", "mix_in", "rows_in", "pos_in", "inv_in", "b_in", "bc_in", "ple_in"))
        ident_ready, zeros_ready, ones_ready, consts = sem("ident_ready"), sem("zeros_ready"), sem("ones_ready"), sem("consts")
        gains_T, gains_ready = sem("gains_T"), sem("gains_ready")
        x_T, act_hi_ready, act_lo_ready = sem("x_T"), sem("act_hi_ready"), sem("act_lo_ready")
        p_T, p_hi_ready, p_lo_ready = sem("p_T"), sem("p_hi_ready"), sem("p_lo_ready")
        ss_ready, ms_ready, rough_ready, rs_ready = sem("ss_ready"), sem("ms_ready"), sem("rough_ready"), sem("rs_ready")
        ga_zeros, ga_hi_ready, ga_lo_ready, ga_done, ga_copied, apre_done = (
            sem(n) for n in ("ga_zeros", "ga_hi_ready", "ga_lo_ready", "ga_done", "ga_copied", "apre_done"))
        neg_abs_ready, log1p_ready, la_ready, la_hi_ready, la_lo_ready, triangles_ready = (
            sem(n) for n in ("neg_abs_ready", "log1p_ready", "la_ready", "la_hi_ready", "la_lo_ready", "triangles_ready"))
        cums_done, decays_ready = sem("cums_done"), sem("decays_ready")
        z_ready = sem("z_ready")
        trig_arg, trig_ready, tables_ready, rope_high = sem("trig_arg"), sem("trig_ready"), sem("tables_ready"), sem("rope_high")
        sq_ready, msq_ready, rough_qk, qk_ready = sem("sq_ready"), sem("msq_ready"), sem("rough_qk"), sem("qk_ready")
        qkT_done, qkT_copied = sem("qkT_done"), sem("qkT_copied")
        gla_ops, glaT_done, glaT_copied = sem("gla_ops"), sem("glaT_done"), sem("glaT_copied")
        scores_done, masked, bias_ready, exp_done, probs_ready = (
            sem("scores_done"), sem("masked"), sem("bias_ready"), sem("exp_done"), sem("probs_ready"))
        aT_done, aT_masked = sem("aT_done"), sem("aT_masked")
        pT_done, pT_copied, pv_done = sem("pT_done"), sem("pT_copied"), sem("pv_done")
        mix_hi_ready, mix_lo_ready = sem("mix_hi_ready"), sem("mix_lo_ready")
        ds_done, states_ready = sem("ds_done"), sem("states_ready")
        gg_nabs, gg_log, gg_logsig, gg_sig, gla_gate = sem("gg_nabs"), sem("gg_log"), sem("gg_logsig"), sem("gg_sig"), sem("gla_gate")
        o_done, o_sq, o_ms, o_rough, o_ready, oT_done = (
            sem("o_done"), sem("o_sq"), sem("o_ms"), sem("o_rough"), sem("o_ready"), sem("oT_done"))
        pp0_copied, pp1_copied, e_ready = sem("pp0_copied"), sem("pp1_copied"), sem("e_ready")
        h_ready, cols_done, tile_done = sem("h_ready"), sem("cols_done"), sem("tile_done")
        relu_done, squared, hidT_done, hid_hi, hid_lo = (
            sem("relu_done"), sem("squared"), sem("hidT_done"), sem("hid_hi"), sem("hid_lo"))
        gate_done, out_ready, stored = sem("gate_done"), sem("out_ready"), sem("stored")
        dve_chain, act_chain, pool_chain = sem("dve_chain"), sem("act_chain"), sem("pool_chain")

        def cols_half(w, k0, n0):
            return w[k0 * P:(k0 + 2) * P, bass.ds(n0, NW)].rearrange("(k p) n -> p k n", p=P)

        def rows_half(w, r0):
            return w[bass.ds(r0, P), :].rearrange("(k p) n -> p k n", p=P)

        def raw_slot(v, k):
            return w_raw[:, v % RAW, :].rearrange("p (k n) -> p k n", k=k)

        def halfmat(buf, v, k):
            return buf[:, v % PAIRS, :].rearrange("p (k n) -> p k n", k=k)

        block = ctx.enter_context(nc.Block())

        @block.sync
        def _(sp):
            def load(v, src):
                if v >= RAW:
                    sp.wait_ge(lo_done, v - RAW + 1)
                nc.sync.dma_start(raw_slot(v, src.shape[1]), src).then_inc(raw_ready[v % RAW], 16)

            def small_loads(j):
                if j == 0:
                    nc.sync.dma_start(w_ga[:, :, :], w_in[:, C_GA:C_GA + LOWRANK].rearrange("(k p) n -> p k n", p=P)).then_inc(ga_in, 16)
                if j == 1:
                    for t in range(T):
                        nc.sync.dma_start(pos_i[:, t:t + 1], positions[t * P:(t + 1) * P].unsqueeze(1)).then_inc(pos_in, 16)
                    nc.sync.dma_start(inv_b[:, :], inv_freq.partition_broadcast(P)).then_inc(inv_in, 16)
                    for t in range(T):
                        nc.sync.dma_start(p_sb[:, t, :], p[t * P:(t + 1) * P, :]).then_inc(p_in, 16)
                if j == 2:
                    nc.sync.dma_start(gain_rows[0:KT, :], g_ffn.rearrange("(k p) -> k p", p=P)).then_inc(rows_in, 16)
                    nc.sync.dma_start(gain_rows[KT:2 * KT, :], g_gate.rearrange("(k p) -> k p", p=P)).then_inc(rows_in, 16)
                    for r in range(2):
                        nc.sync.dma_start(a2[r * LOWRANK:(r + 1) * LOWRANK, :], w_a2).then_inc(a2_in, 16)
                    nc.sync.dma_start(b_a_b[:, :], b_a.partition_broadcast(P)).then_inc(b_in, 16)
                if j == 3:
                    nc.sync.dma_start(g_mq_b[:, :], g_mq.partition_broadcast(P)).then_inc(bc_in, 16)
                    nc.sync.dma_start(g_mk_b[:, :], g_mk.partition_broadcast(P)).then_inc(bc_in, 16)
                    nc.sync.dma_start(g_gla_b[:, :], g_gla.partition_broadcast(P)).then_inc(bc_in, 16)

            for t in range(T):
                nc.sync.dma_start(h[:, t, :], x[t * P:(t + 1) * P, :]).then_inc(x_in[t], 16)
            for i, n0 in enumerate(GROUP_COLS):
                if i == 5:
                    nc.sync.dma_start(g_ple_b[:, :], g_ple.partition_broadcast(P)).then_inc(ple_in, 16)
                    for n in range(2):
                        load(H_PP + n, cols_half(w_pp, 0, n * NW))
                for j in range(4):
                    load(H_GROUP[i] + j, cols_half(w_in, 2 * j, n0))
                    if i == 0:
                        small_loads(j)
            for k in range(KT):
                load(H_OUT + k, rows_half(w_out, k * P))
            for j in range(4):
                load(H_UP0 + j, cols_half(w_up, 2 * j, 0))
            with sp.Fori(1, GROUPS) as g:
                for j in range(LOOP_HALVES):
                    v = H_LOOP + j
                    sp.wait_ge(lo_done, LOOP_HALVES * g + (v - RAW + 1 - LOOP_HALVES))
                    src = cols_half(w_up, 2 * j, g * NW) if j < 4 else rows_half(w_down, g * NW + ((j - 4) * P - NW))
                    nc.sync.dma_start(raw_slot(v, src.shape[1]), src).then_inc(raw_ready[v % RAW], 16)
            for j in range(4):
                load(H_DOWN_LAST + j, rows_half(w_down, (GROUPS - 1) * NW + j * P))
            for n in range(2):
                for j in range(4):
                    load(H_GATE + 4 * n + j, cols_half(w_gate, 2 * j, n * NW))
            for i, (n, t, c0, c1) in enumerate(GATE_PIECES):
                sp.wait_ge(out_ready, i + 1)
                nc.sync.dma_start(out[t * P:(t + 1) * P, n * NW + c0:n * NW + c1],
                                  gate_tmp[:, n, t, c0:c1]).then_inc(stored, 16)
            sp.wait_ge(stored, 16 * len(GATE_PIECES))

        @block.scalar
        def _(act):
            def split(v):
                if v >= PAIRS:
                    act.wait_ge(half_used, v - PAIRS + 1)
                act.wait_ge(raw_ready[v % RAW], 16 * (v // RAW + 1))
                nc.scalar.activation(w_hi[:, v % PAIRS, :], w_raw[:, v % RAW, :], ACT.Copy).then_inc(hi_done, 1)

            links = [0]

            def link(ins):
                links[0] += 1
                ins.then_inc(act_chain, 1)
                act.wait_ge(act_chain, links[0])

            def rough_rsqrt(dst, src, s):
                link(nc.scalar.activation(dst, src, ACT.Ln))
                nc.scalar.activation(dst, dst, ACT.Exp, scale=-0.5).then_inc(s, 1)

            def group_out(i):
                act.wait_ge(half_used, H_GROUP[i] + 4)
                if i == 0:
                    act.wait_ge(rs_ready, 1)
                for t in range(T):
                    last = nc.scalar.activation(z[:, i, t, :], ps[:, 2 * (i % 2) + t, :], ACT.Copy, scale=rs[:, t:t + 1])
                last.then_inc(z_ready, 1)

            def high_transposed(i, b):
                act.wait_ge(x_T, 4 * i + b + 1)
                for k in range(2):
                    c = KT * i + 2 * b + k
                    last = nc.scalar.activation(act_hi[:, 2 * b + k, :], ps[:, T_BANK[i] + b, k * SEQ:(k + 1) * SEQ], ACT.Copy,
                                                scale=gains[:, c:c + 1])
                last.then_inc(act_hi_ready, 1)

            nc.scalar.dma_start(mix_rows[:, :], g_mix.rearrange("(k p) -> k p", p=P)).then_inc(mix_in, 16)
            nc.scalar.preload_act_table(ACT.Sin)
            act.wait_ge(gains_ready, 1)
            high_transposed(0, 0)
            split(0)
            high_transposed(0, 1)
            split(1)
            high_transposed(0, 2)
            high_transposed(0, 3)
            split(2)
            act.wait_ge(ga_in, 16)
            act.wait_ge(ga_zeros, 1)
            nc.scalar.activation(ga_pack[:, :, 0:LOWRANK], w_ga[:, :, :], ACT.Copy).then_inc(ga_hi_ready, 1)
            split(3)
            for t in range(T):
                nc.scalar.activation(scratch[:, t * D:(t + 1) * D], h[:, t, :], ACT.Square,
                                     accum_out=ss[:, t:t + 1]).then_inc(ss_ready, 1)
            act.wait_ge(consts, 1)
            nc.scalar.activation(triangles[:, 0, :], tri[:, :], ACT.Copy).then_inc(triangles_ready, 1)
            nc.scalar.activation(triangles[:, 1, :], rest[:, :], ACT.Copy).then_inc(triangles_ready, 1)
            act.wait_ge(ga_done, 1)
            nc.scalar.activation(ga_T[:, :], ps[0:2 * LOWRANK, 4, 0:SEQ], ACT.Copy).then_inc(ga_copied, 1)
            act.wait_ge(p_T, 1)
            nc.scalar.activation(p_hi[:, :, :], ps[:, 2, :].rearrange("p (k s) -> p k s", k=2), ACT.Copy).then_inc(p_hi_ready, 1)
            split(4)
            act.wait_ge(trig_arg, 1)
            nc.scalar.activation(sin_t[:, :], angle[:, :], ACT.Sin).then_inc(trig_ready, 1)
            nc.scalar.activation(cos_t[:, :], turns[:, :], ACT.Sin).then_inc(trig_ready, 1)
            nc.scalar.preload_act_table_set("natural_log_exp_and_others")
            act.wait_ge(ms_ready, 1)
            rough_rsqrt(rs[:, 0:T], ms[:, 0:T], rough_ready)
            split(5)
            split(6)
            act.wait_ge(neg_abs_ready, 1)
            act.wait_ge(ones_ready, 1)
            link(nc.scalar.activation(la_nabs[:, :, :], la_nabs[:, :, :], ACT.Exp))
            nc.scalar.activation(la_nabs[:, :, :], la_nabs[:, :, :], ACT.Ln, bias=one[:, 0:1]).then_inc(log1p_ready, 1)
            act.wait_ge(la_ready, 1)
            nc.scalar.activation(la_hi[:, :, :], la[:, :, :], ACT.Copy).then_inc(la_hi_ready, 1)
            split(7)
            group_out(0)
            split(8)
            act.wait_ge(z_ready, 1)
            nc.scalar.activation(squares, z[:, Z_MQ, :, :].rearrange("p t n -> p (t n)"), ACT.Square).then_inc(sq_ready, 1)
            split(9)
            act.wait_ge(cums_done, 1)
            nc.scalar.activation(dec[:, :, :, :].rearrange("p t b n -> p t (b n)"), ps[:, 6:8, :], ACT.Exp).then_inc(decays_ready, 1)
            nc.scalar.activation(inv_dec[:, :, :], ps[:, 6:8, 0:256], ACT.Exp, scale=-1.0).then_inc(decays_ready, 1)
            nc.scalar.activation(decay[:, :, :, :].rearrange("p a t c -> p (a t c)"), ps[:, 4, 0:8], ACT.Exp).then_inc(decays_ready, 1)
            act.wait_ge(msq_ready, 1)
            rough_rsqrt(rs_q[:, :], ss_q[:, :], rough_qk)
            split(10)
            split(11)
            group_out(1)
            act.wait_ge(z_ready, 2)
            act.wait_ge(msq_ready, 1)
            nc.scalar.activation(squares, z[:, Z_MK, :, :].rearrange("p t n -> p (t n)"), ACT.Square).then_inc(sq_ready, 1)
            split(12)
            act.wait_ge(qkT_done, 1)
            nc.scalar.activation(q_T.rearrange("p (a h) s -> p a (h s)", a=2), ps[:, 4:6, :], ACT.Copy).then_inc(qkT_copied, 1)
            split(13)
            act.wait_ge(msq_ready, 2)
            rough_rsqrt(rs_k[:, :], ss_k[:, :], rough_qk)
            split(14)
            split(15)
            group_out(2)
            split(16)
            act.wait_ge(qkT_done, 2)
            nc.scalar.activation(k_T.rearrange("p (a h) s -> p a (h s)", a=2), ps[:, 6:8, :], ACT.Copy).then_inc(qkT_copied, 1)
            split(17)
            split(18)
            act.wait_ge(glaT_done, 1)
            nc.scalar.activation(qd_T[:, :, :, :].rearrange("p a t c -> p (a t c)"), ps[:, 4, :], ACT.Copy).then_inc(glaT_copied, 1)
            nc.scalar.activation(ki_T[:, :, :, :].rearrange("p a t c -> p (a t c)"), ps[:, 5, :], ACT.Copy).then_inc(glaT_copied, 1)
            split(19)
            group_out(3)
            split(20)

            def softmax_exp(i):
                act.wait_ge(bias_ready, i + 1)
                for hd in (2 * i, 2 * i + 1):
                    for t in range(T):
                        c = 2 * hd + t
                        s = slice(0, P) if t == 0 else slice(P, 3 * P)
                        nc.scalar.activation(probs[:, hd, s], probs[:, hd, s], ACT.Exp, scale=rs_q[:, c:c + 1],
                                             bias=nbias[:, c:c + 1], accum_out=rowsum[:, c:c + 1]).then_inc(exp_done, 1)

            softmax_exp(0)
            split(21)
            softmax_exp(1)
            split(22)
            act.wait_ge(gg_nabs, 1)
            link(nc.scalar.activation(silu_nabs, silu_nabs, ACT.Exp))
            nc.scalar.activation(silu_log, silu_nabs, ACT.Ln, bias=one[:, 0:1]).then_inc(gg_log, 1)
            group_out(4)
            split(23)
            split(24)
            act.wait_ge(half_used, H_PP + 1)
            nc.scalar.activation(e[:, :, 0:NW], ps[:, 2:4, :], ACT.Copy).then_inc(pp0_copied, 1)
            act.wait_ge(gg_logsig, 1)
            nc.scalar.activation(silu_nabs, silu_log, ACT.Exp).then_inc(gg_sig, 1)
            split(25)
            act.wait_ge(o_done, 1)
            nc.scalar.activation(o_squares.rearrange("p (b n) -> p b n", b=2), ps[:, 4:6, :], ACT.Square).then_inc(o_sq, 1)
            split(26)
            act.wait_ge(o_ms, 1)
            rough_rsqrt(rs_o[:, :], ss_o[:, :], o_rough)
            act.wait_ge(pT_done, 1)
            nc.scalar.activation(probs_T[:, 0:2, :], ps[:, 6:8, 0:384], ACT.Copy).then_inc(pT_copied, 1)
            split(27)
            act.wait_ge(pT_done, 2)
            nc.scalar.activation(probs_T[:, 2:4, :], ps[:, 6:8, 0:384], ACT.Copy).then_inc(pT_copied, 1)
            act.wait_ge(oT_done, 1)
            for b in range(2):
                nc.scalar.activation(mix_hi[:, 2 * b:2 * b + 2, :], ps[:, 4 + b, :].rearrange("p (k s) -> p k s", k=2),
                                     ACT.Copy).then_inc(mix_hi_ready, 1)
            split(28)
            group_out(5)
            split(29)
            split(30)
            act.wait_ge(pv_done, 1)
            for b in range(2):
                nc.scalar.activation(mix_hi[:, 4 + 2 * b:6 + 2 * b, :], ps[:, 6 + b, :].rearrange("p (k s) -> p k s", k=2),
                                     ACT.Copy).then_inc(mix_hi_ready, 1)
            split(31)
            act.wait_ge(pp1_copied, 1)
            act.wait_ge(gla_gate, T)
            for t in range(T):
                nc.scalar.activation(scratch[:, t * D:(t + 1) * D], e[:, t, :], ACT.Square,
                                     accum_out=ss[:, 6 + t:7 + t]).then_inc(ss_ready, 1)
            act.wait_ge(ms_ready, 2)
            rough_rsqrt(rs[:, 6:8], ms[:, 6:8], rough_ready)
            split(32)
            split(33)

            def residual(i, v):
                for v4 in range(v, v + 3):
                    split(v4)
                for b in range(4):
                    high_transposed(i, b)
                split(v + 3)
                for t in range(T):
                    nc.scalar.activation(scratch[:, t * D:(t + 1) * D], h[:, t, :], ACT.Square,
                                         accum_out=ss[:, 2 * i + t:2 * i + t + 1]).then_inc(ss_ready, 1)
                act.wait_ge(ms_ready, i + 2)
                rough_rsqrt(rs[:, 2 * i:2 * i + T], ms[:, 2 * i:2 * i + T], rough_ready)

            def relu_out(need, bank=0):
                act.wait_ge(half_used, need)
                for t in range(T):
                    nc.scalar.activation(hidden[:, t, :], ps[:, bank + t, :], ACT.Relu, scale=rs[:, 2 + t:3 + t]).then_inc(relu_done, 1)

            residual(1, H_UP0)
            act.wait_ge(rs_ready, 3)

            def ffn_group(g, first=False):
                for j in range(LOOP_HALVES):
                    v = H_LOOP + j
                    act.wait_ge(half_used, LOOP_HALVES * g + (v - PAIRS + 1 - LOOP_HALVES))
                    act.wait_ge(raw_ready[v % RAW], 16 * g + 16 * (v // RAW))
                    nc.scalar.activation(w_hi[:, v % PAIRS, :], w_raw[:, v % RAW, :], ACT.Copy).then_inc(hi_done, 1)
                    if j == 2 and first:
                        relu_out(H_LOOP, bank=2)
                    if j == 3:
                        for b in range(2):
                            act.wait_ge(hidT_done, 2 * g + (b - 1))
                            nc.scalar.activation(mix_hi[:, 2 * b:2 * b + 2, :], ps[:, 2 + b, :].rearrange("p (k s) -> p k s", k=2),
                                                 ACT.Copy).then_inc(hid_hi, 1)
                relu_out(LOOP_HALVES * g + (H_LOOP + 4 - LOOP_HALVES))

            ffn_group(1, first=True)
            with act.Fori(2, GROUPS) as g:
                ffn_group(g)
            split(H_DOWN_LAST)
            split(H_DOWN_LAST + 1)
            for b in range(2):
                act.wait_ge(hidT_done, 2 * GROUPS + b - 1)
                nc.scalar.activation(mix_hi[:, 4 + 2 * b:6 + 2 * b, :], ps[:, 2 + b, :].rearrange("p (k s) -> p k s", k=2),
                                     ACT.Copy).then_inc(hid_hi, 1)
            split(H_DOWN_LAST + 2)
            split(H_DOWN_LAST + 3)
            residual(2, H_GATE)
            for v in range(H_GATE + 4, H_END):
                split(v)
            nc.scalar.preload_act_table(ACT.Sigmoid)
            act.wait_ge(rs_ready, 4)
            act.wait_ge(half_used, H_GATE + 4)
            for n, t, c0, c1 in GATE_PIECES:
                if n == 1:
                    act.wait_ge(tile_done, t + 1)
                nc.scalar.activation(gate_tmp[:, n, t, c0:c1], ps[:, 4 + 2 * n + t, c0:c1], ACT.Sigmoid,
                                     scale=rs[:, 4 + t:5 + t]).then_inc(gate_done, 1)

        @block.vector
        def _(dve):
            links = [0]

            def link(ins):
                links[0] += 1
                ins.then_inc(dve_chain, 1)
                dve.wait_ge(dve_chain, links[0])

            def split(v):
                dve.wait_ge(hi_done, v + 1)
                nc.vector.tensor_tensor(w_lo[:, v % PAIRS, :], w_raw[:, v % RAW, :], w_hi[:, v % PAIRS, :].bitcast(F32),
                                        ALU.subtract).then_inc(lo_done, 1)

            def refine(y, m, tmp):
                link(nc.vector.tensor_tensor(tmp, y, y, ALU.mult))
                link(nc.vector.tensor_tensor(tmp, tmp, m, ALU.mult))
                link(nc.vector.tensor_scalar(tmp, tmp, -0.5, 1.5, ALU.mult, ALU.add))
                return nc.vector.tensor_tensor(y, y, tmp, ALU.mult)

            def mean_eps(dst, src, width, s):
                nc.vector.tensor_scalar(dst, src, 1.0 / width, EPS, ALU.mult, ALU.add).then_inc(s, 1)

            nc.vector.memset(zeros[:, :], 0.0).then_inc(zeros_ready, 1)
            nc.vector.memset(one[:, :], 1.0).then_inc(ones_ready, 1)
            nc.vector.memset(ga_pack[:, :, :].bitcast(F32), 0.0).then_inc(ga_zeros, 1)
            dve.wait_ge(gains_T, 1)
            nc.vector.tensor_copy(gains[:, 0:KT], ps[:, 3, 0:KT]).then_inc(gains_ready, 1)
            dve.wait_ge(gains_ready, 1)

            def low_transposed(i, b):
                dve.wait_ge(act_hi_ready, 4 * i + b + 1)
                for k in range(2):
                    c = KT * i + 2 * b + k
                    last = nc.vector.scalar_tensor_tensor(
                        act_lo[:, 2 * b + k, :], ps[:, T_BANK[i] + b, k * SEQ:(k + 1) * SEQ], gains[:, c:c + 1],
                        act_hi[:, 2 * b + k, :].bitcast(F32), ALU.mult, ALU.subtract)
                last.then_inc(act_lo_ready, 1)

            low_transposed(0, 0)
            split(0)
            low_transposed(0, 1)
            split(1)
            low_transposed(0, 2)
            split(2)
            low_transposed(0, 3)
            dve.wait_ge(ga_hi_ready, 1)
            nc.vector.tensor_tensor(ga_pack[:, :, LOWRANK:2 * LOWRANK], w_ga[:, :, :], ga_pack[:, :, 0:LOWRANK].bitcast(F32),
                                    ALU.subtract).then_inc(ga_lo_ready, 1)
            split(3)
            dve.wait_ge(pos_in, 16 * T)
            dve.wait_ge(inv_in, 16)
            link(nc.vector.tensor_copy(pos_f[:, :], pos_i[:, :]))
            for t in range(T):
                last = nc.vector.tensor_scalar(angle[:, t * 64:(t + 1) * 64], inv_b[:, :], pos_f[:, t:t + 1], None, ALU.mult)
            link(last)
            link(nc.vector.tensor_scalar(turns[:, :], angle[:, :], 1.0 / TWO_PI, ROUND, ALU.mult, ALU.add))
            link(nc.vector.tensor_scalar(turns[:, :], turns[:, :], -ROUND, None, ALU.add))
            for part in (PI_A, PI_B, PI_C):
                link(nc.vector.scalar_tensor_tensor(angle[:, :], turns[:, :], -part, angle[:, :], ALU.mult, ALU.add))
            link(nc.vector.tensor_scalar(angle[:, :], angle[:, :], PI_BELOW, -PI_BELOW, ALU.min, ALU.max))
            link(nc.vector.scalar_tensor_tensor(turns[:, :], angle[:, :], -1.0, angle[:, :], ALU.mult, ALU.min))
            nc.vector.tensor_scalar(turns[:, :], turns[:, :], HALF_PI, None, ALU.add).then_inc(trig_arg, 1)

            dve.wait_ge(ss_ready, T)
            mean_eps(ms[:, 0:T], ss[:, 0:T], D, ms_ready)
            dve.wait_ge(gains_T, 2)
            nc.vector.tensor_copy(gains[:, KT:3 * KT], ps[:, 3, KT:3 * KT]).then_inc(gains_ready, 1)
            dve.wait_ge(p_hi_ready, 1)
            nc.vector.tensor_tensor(p_lo[:, :, :], ps[:, 2, :].rearrange("p (k s) -> p k s", k=2), p_hi[:, :, :].bitcast(F32),
                                    ALU.subtract).then_inc(p_lo_ready, 1)
            split(4)
            dve.wait_ge(rough_ready, 1)
            refine(rs[:, 0:T], ms[:, 0:T], nt[:, 0:T]).then_inc(rs_ready, 1)
            split(5)
            dve.wait_ge(rs_ready, 1)
            dve.wait_ge(apre_done, 1)
            dve.wait_ge(b_in, 16)
            for t in range(T):
                last = nc.vector.scalar_tensor_tensor(la[:, t, :], ps[:, 5, t * 256:(t + 1) * 256], rs[:, t:t + 1], b_a_b[:, :],
                                                      ALU.mult, ALU.add)
            link(last)
            nc.vector.scalar_tensor_tensor(la_nabs[:, :, :], la[:, :, :], -1.0, la[:, :, :], ALU.mult, ALU.min).then_inc(neg_abs_ready, 1)
            split(6)
            dve.wait_ge(log1p_ready, 1)
            nc.vector.scalar_tensor_tensor(la[:, :, :], la[:, :, :], 0.0, la_nabs[:, :, :], ALU.min, ALU.subtract).then_inc(la_ready, 1)
            dve.wait_ge(la_hi_ready, 1)
            nc.vector.tensor_tensor(la_lo[:, :, :], la[:, :, :], la_hi[:, :, :].bitcast(F32), ALU.subtract).then_inc(la_lo_ready, 1)
            split(7)

            def mean_square(i, ssd):
                dve.wait_ge(sq_ready, i + 1)
                link(nc.vector.tensor_reduce(ssd[:, :].rearrange("p (h t) -> p t h", h=HEADS),
                                             squares.rearrange("p (t h d) -> p t h d", t=T, h=HEADS), AXIS_X, ALU.add))
                mean_eps(ssd[:, :], ssd[:, :], HD, msq_ready)

            def rope_low(i, tab):
                zz = z[:, Z_MQ + i, :, :].rearrange("p t (h d) -> p t h d", h=HEADS)
                x1, x2 = zz[:, :, :, 0:64], zz[:, :, :, 64:128]
                if i:
                    dve.wait_ge(qk_ready, 2 * i)
                bc = lambda j: tab[:, j, :, :].unsqueeze(2).broadcast_to([P, T, HEADS, 64])
                nc.vector.tensor_tensor(rope_tmp[:, 0], x1, bc(0), ALU.mult)
                link(nc.vector.tensor_tensor(rope_tmp[:, 1], x2, bc(1), ALU.mult))
                dve.wait_ge(rope_high, 2 * (i + 1))
                nc.vector.tensor_tensor(x1, rope_tmp[:, 0], rope_tmp[:, 1], ALU.subtract).then_inc(qk_ready, 1)
                nc.vector.tensor_tensor(x2, rope_tmp[:, 2], rope_tmp[:, 3], ALU.add).then_inc(qk_ready, 1)

            split(8)
            mean_square(0, ss_q)
            dve.wait_ge(tables_ready, 1)
            split(9)
            rope_low(0, rope_q)
            dve.wait_ge(rough_qk, 1)
            link(refine(rs_q[:, :], ss_q[:, :], nq[:, :]))
            link(nc.vector.tensor_scalar(rs_q[:, :], rs_q[:, :], HD ** -0.5, None, ALU.mult))
            split(10)
            split(11)
            mean_square(1, ss_k)
            split(12)
            rope_low(1, rope_k)
            split(13)
            dve.wait_ge(rough_qk, 2)
            link(refine(rs_k[:, :], ss_k[:, :], nq[:, :]))
            dve.wait_ge(qk_ready, 4)
            for t in range(T):
                kk = z[:, Z_MK, t, :].rearrange("p (h d) -> p h d", h=HEADS)
                nc.vector.tensor_tensor(kk, kk, rs_k[:, t:8:2].unsqueeze(2).broadcast_to([P, HEADS, HD]), ALU.mult).then_inc(qk_ready, 1)
            split(14)
            split(15)
            split(16)
            dve.wait_ge(z_ready, 3)
            dve.wait_ge(decays_ready, 3)
            gq, gk = z[:, Z_GQK, :, 0:256], z[:, Z_GQK, :, 256:512]
            nc.vector.scalar_tensor_tensor(dec[:, :, 0, :], gq, DK ** -0.5, dec[:, :, 0, :], ALU.mult, ALU.mult).then_inc(gla_ops, 1)
            nc.vector.tensor_tensor(inv_dec[:, :, :], gk, inv_dec[:, :, :], ALU.mult).then_inc(gla_ops, 1)
            nc.vector.tensor_tensor(dec[:, :, 1, :], gk, dec[:, :, 1, :], ALU.mult).then_inc(gla_ops, 1)
            split(17)
            split(18)
            split(19)

            def mask_scores(hd):
                dve.wait_ge(scores_done, hd + 1)
                b = 4 + (hd + 2) % 4
                for t in range(T):
                    lo_c, hi_c = (0, P) if t == 0 else (P, 3 * P)
                    nc.vector.tensor_tensor_reduce(
                        out=probs[:, hd, lo_c:hi_c], in0=ps[:, b, lo_c:hi_c], in1=causal[:, P if t == 0 else 0:2 * P],
                        scale=1.0, scalar=-3e38, op0=ALU.add, op1=ALU.max,
                        accum_out=qmax[:, 2 * hd + t:2 * hd + t + 1]).then_inc(masked, 1)

            def softmax_bias(i):
                c = slice(4 * i, 4 * i + 4)
                dve.wait_ge(masked, 4 * (i + 1))
                nc.vector.scalar_tensor_tensor(nbias[:, c], qmax[:, c], -1.0, rs_q[:, c], ALU.mult, ALU.mult).then_inc(bias_ready, 1)

            def normalise(i):
                c = slice(4 * i, 4 * i + 4)
                dve.wait_ge(exp_done, 4 * (i + 1))
                link(nc.vector.reciprocal(rinv[:, c], rowsum[:, c]))
                for hd in (2 * i, 2 * i + 1):
                    for t in range(T):
                        lo_c, hi_c = (0, P) if t == 0 else (P, 3 * P)
                        last = nc.vector.tensor_scalar(probs[:, hd, lo_c:hi_c], probs[:, hd, lo_c:hi_c],
                                                       rinv[:, 2 * hd + t:2 * hd + t + 1], None, ALU.mult)
                last.then_inc(probs_ready, 1)

            mask_scores(0)
            mask_scores(1)
            softmax_bias(0)
            split(20)
            mask_scores(2)
            mask_scores(3)
            softmax_bias(1)
            split(21)
            dve.wait_ge(aT_done, 2)
            dve.wait_ge(consts, 1)
            for b in range(2):
                nc.vector.copy_predicated(a_T[:, b, :, :, :].rearrange("p t a c -> p (t a) c"),
                                          tri[:, :].bitcast(I32).unsqueeze(1).broadcast_to([P, 4, P]),
                                          ps[:, 6 + b, :].rearrange("p (m c) -> p m c", m=4)).then_inc(aT_masked, 1)
            dve.wait_ge(z_ready, 4)
            gg = z[:, Z_GG, :, :].rearrange("p t n -> p (t n)")
            nc.vector.scalar_tensor_tensor(silu_nabs, gg, -1.0, gg, ALU.mult, ALU.min).then_inc(gg_nabs, 1)
            split(22)
            normalise(0)
            split(23)
            dve.wait_ge(ds_done, 1)
            link(nc.vector.tensor_copy(state[:, 0, :, :], ps[:, 6, 0:256].rearrange("p (a v) -> p a v", a=2)))
            for n, bank, c0 in ((1, 7, 0), (2, 6, 256)):
                for a in range(2):
                    last = nc.vector.scalar_tensor_tensor(
                        state[:, n, a, :], state[:, n - 1, a, :], decay[:, a, n // 2, n % 2:n % 2 + 1],
                        ps[:, bank, c0 + a * DV:c0 + (a + 1) * DV], ALU.mult, ALU.add)
                if n == 1:
                    link(last)
            last.then_inc(states_ready, 1)
            dve.wait_ge(gg_log, 1)
            nc.vector.scalar_tensor_tensor(silu_log, gg, 0.0, silu_log, ALU.min, ALU.subtract).then_inc(gg_logsig, 1)
            normalise(1)
            split(24)
            split(25)
            dve.wait_ge(half_used, H_PP + 2)
            nc.vector.tensor_copy(e[:, :, NW:D], ps[:, 0:2, :]).then_inc(pp1_copied, 1)
            dve.wait_ge(o_sq, 1)
            link(nc.vector.tensor_reduce(ss_o[:, :], o_squares.rearrange("p (m d) -> p m d", d=DV), AXIS_X, ALU.add))
            mean_eps(ss_o[:, :], ss_o[:, :], DV, o_ms)
            split(26)
            dve.wait_ge(o_rough, 1)
            link(refine(rs_o[:, :], ss_o[:, :], nq[:, :]))
            dve.wait_ge(gla_gate, T)
            for par in range(2):
                ov = o_gla.rearrange("p t (a r v) -> p t a r v", a=2, r=2)[:, :, :, par, :]
                gv_ = z[:, Z_GG, :, :].rearrange("p t (a r v) -> p t a r v", a=2, r=2)[:, :, :, par, :]
                link(nc.vector.tensor_tensor(
                    ov, ps[:, 4 + par, :].rearrange("p (t a v) -> p t a v", t=T, a=2),
                    rs_o[:, 4 * par:4 * par + 4].rearrange("p (t a) -> p t a", t=T).unsqueeze(3).broadcast_to([P, T, 2, DV]), ALU.mult))
                nc.vector.tensor_tensor(ov, ov, gv_, ALU.mult).then_inc(o_ready, 1)
            split(27)

            def mix_low(b):
                dve.wait_ge(mix_hi_ready, b + 1)
                nc.vector.tensor_tensor(mix_lo[:, 2 * b:2 * b + 2, :], ps[:, 4 + b, :].rearrange("p (k s) -> p k s", k=2),
                                        mix_hi[:, 2 * b:2 * b + 2, :].bitcast(F32), ALU.subtract).then_inc(mix_lo_ready, 1)

            mix_low(0)
            mix_low(1)
            split(28)
            split(29)
            split(30)
            mix_low(2)
            mix_low(3)
            split(31)
            dve.wait_ge(ss_ready, 2 * T)
            mean_eps(ms[:, 6:8], ss[:, 6:8], D, ms_ready)
            split(32)
            dve.wait_ge(rough_ready, 2)
            refine(rs[:, 6:8], ms[:, 6:8], nt[:, 6:8]).then_inc(rs_ready, 1)
            dve.wait_ge(rs_ready, 2)
            dve.wait_ge(ple_in, 16)
            for t in range(T):
                last = nc.vector.scalar_tensor_tensor(e[:, t, :], e[:, t, :], rs[:, 6 + t:7 + t], g_ple_b[:, :], ALU.mult, ALU.mult)
            last.then_inc(e_ready, 1)
            split(33)

            def residual(i, v, bank):
                split(v)
                split(v + 1)
                for n in range(2):
                    for t in range(T):
                        if (n, t) == (1, T - 1):
                            dve.wait_ge(half_used, v)
                        else:
                            dve.wait_ge(cols_done, 3 * (i - 1) + 2 * n + t + 1)
                        nc.vector.tensor_tensor(h[:, t, n * NW:(n + 1) * NW], ps[:, bank(t, n), :],
                                                h[:, t, n * NW:(n + 1) * NW], ALU.add).then_inc(h_ready, 1)
                for b in range(4):
                    low_transposed(i, b)
                    if b == 1:
                        split(v + 2)
                split(v + 3)
                dve.wait_ge(ss_ready, T * (i + 2))
                mean_eps(ms[:, 2 * i:2 * i + T], ss[:, 2 * i:2 * i + T], D, ms_ready)
                dve.wait_ge(rough_ready, i + 2)
                refine(rs[:, 2 * i:2 * i + T], ms[:, 2 * i:2 * i + T], nt[:, 2 * i:2 * i + T]).then_inc(rs_ready, 1)

            residual(1, H_UP0, lambda t, n: 2 * t + n)

            def square(t, wait):
                dve.wait_ge(relu_done, wait)
                nc.vector.tensor_tensor(hidden[:, t, :], hidden[:, t, :], hidden[:, t, :], ALU.mult).then_inc(squared, 1)

            def ffn_group(g, first=False):
                for j in range(LOOP_HALVES):
                    v = H_LOOP + j
                    dve.wait_ge(hi_done, LOOP_HALVES * g + (v + 1 - LOOP_HALVES))
                    nc.vector.tensor_tensor(w_lo[:, v % PAIRS, :], w_raw[:, v % RAW, :], w_hi[:, v % PAIRS, :].bitcast(F32),
                                            ALU.subtract).then_inc(lo_done, 1)
                    if j == 2 and first:
                        for t in range(T):
                            square(t, t + 1)
                    if j == 3:
                        for b in range(2):
                            dve.wait_ge(hid_hi, 2 * g + (b - 1))
                            nc.vector.tensor_tensor(mix_lo[:, 2 * b:2 * b + 2, :], ps[:, 2 + b, :].rearrange("p (k s) -> p k s", k=2),
                                                    mix_hi[:, 2 * b:2 * b + 2, :].bitcast(F32), ALU.subtract).then_inc(hid_lo, 1)
                for t in range(T):
                    square(t, T * g + (t + 1))

            ffn_group(1, first=True)
            with dve.Fori(2, GROUPS) as g:
                ffn_group(g)
            split(H_DOWN_LAST)
            split(H_DOWN_LAST + 1)
            for b in range(2):
                dve.wait_ge(hid_hi, 2 * GROUPS + b - 1)
                nc.vector.tensor_tensor(mix_lo[:, 4 + 2 * b:6 + 2 * b, :], ps[:, 2 + b, :].rearrange("p (k s) -> p k s", k=2),
                                        mix_hi[:, 4 + 2 * b:6 + 2 * b, :].bitcast(F32), ALU.subtract).then_inc(hid_lo, 1)
            split(H_DOWN_LAST + 2)
            split(H_DOWN_LAST + 3)
            residual(2, H_GATE, lambda t, n: 4 + 2 * t + n)
            for v in range(H_GATE + 4, H_END):
                split(v)
            dve.wait_ge(e_ready, 1)
            for pieces in ([0], [1], [2], [3, 4]):
                views = []
                for i in pieces:
                    n, t, c0, c1 = GATE_PIECES[i]
                    gt, columns = gate_tmp[:, n, t, c0:c1], slice(n * NW + c0, n * NW + c1)
                    views.append((gt, h[:, t, columns]))
                    dve.wait_ge(gate_done, i + 1)
                    last = nc.vector.tensor_tensor(gt, gt, e[:, t, columns], ALU.mult)
                link(last)
                for gt, ht in views:
                    nc.vector.tensor_tensor(gt, gt, ht, ALU.add).then_inc(out_ready, 1)

        @block.gpsimd
        def _(pool):
            links = [0]

            def link(ins):
                links[0] += 1
                ins.then_inc(pool_chain, 1)
                pool.wait_ge(pool_chain, links[0])

            link(nc.gpsimd.memset(ident[:, :], 0.0))
            nc.gpsimd.affine_select(out=ident[:, :], in_=ident[:, :], compare_op=ALU.not_equal, fill=1.0, base=0,
                                    pattern=[[-1, P]], channel_multiplier=1).then_inc(ident_ready, 1)
            nc.gpsimd.memset(tri[:, :], 1.0 / TAU).then_inc(pool_chain, 1)
            nc.gpsimd.memset(chunk_sum[:, :], 0.0).then_inc(pool_chain, 1)
            nc.gpsimd.memset(causal[:, :], 0.0).then_inc(pool_chain, 1)
            nc.gpsimd.memset(a_T[:, :, :, :, :], 0.0).then_inc(pool_chain, 1)
            links[0] += 4
            link(nc.gpsimd.memset(rest[:, :], 1.0 / TAU))
            nc.gpsimd.affine_select(out=tri[:, :], in_=tri[:, :], compare_op=ALU.is_ge, fill=0.0, base=0,
                                    pattern=[[1, P]], channel_multiplier=-1).then_inc(pool_chain, 1)
            nc.gpsimd.affine_select(out=causal[:, P:2 * P], in_=causal[:, P:2 * P], compare_op=ALU.is_ge, fill=MASKED, base=0,
                                    pattern=[[-1, P]], channel_multiplier=1).then_inc(pool_chain, 1)
            links[0] += 2
            link(nc.gpsimd.affine_select(out=rest[:, :], in_=rest[:, :], compare_op=ALU.is_gt, fill=0.0, base=0,
                                         pattern=[[-1, P]], channel_multiplier=1))
            link(nc.gpsimd.memset(tri[0:CHUNK, CHUNK:P], 0.0))
            link(nc.gpsimd.memset(rest[CHUNK:P, 0:CHUNK], 0.0))
            link(nc.gpsimd.memset(chunk_sum[0:CHUNK, 0:1], 1.0 / TAU))
            nc.gpsimd.memset(chunk_sum[CHUNK:P, 1:2], 1.0 / TAU).then_inc(consts, 1)
            pool.wait_ge(consts, 1)
            pool.wait_ge(trig_ready, 2)
            pool.wait_ge(bc_in, 16 * 3)
            for tab, gb in ((rope_q, g_mq_b), (rope_k, g_mk_b)):
                for j, (trig, g0) in enumerate(((cos_t, 0), (sin_t, 64), (cos_t, 64), (sin_t, 0))):
                    last = nc.gpsimd.tensor_tensor(tab[:, j, :, :], trig[:, :].rearrange("p (t d) -> p t d", t=T),
                                                   gb[:, g0:g0 + 64].unsqueeze(1).broadcast_to([P, T, 64]), ALU.mult)
            last.then_inc(tables_ready, 1)
            pool.wait_ge(tables_ready, 1)
            for i, tab in ((0, rope_q), (1, rope_k)):
                pool.wait_ge(z_ready, i + 1)
                zz = z[:, Z_MQ + i, :, :].rearrange("p t (h d) -> p t h d", h=HEADS)
                bc = lambda j: tab[:, j, :, :].unsqueeze(2).broadcast_to([P, T, HEADS, 64])
                if i:
                    pool.wait_ge(qk_ready, 2)
                nc.gpsimd.tensor_tensor(rope_tmp[:, 2], zz[:, :, :, 64:128], bc(2), ALU.mult).then_inc(rope_high, 1)
                nc.gpsimd.tensor_tensor(rope_tmp[:, 3], zz[:, :, :, 0:64], bc(3), ALU.mult).then_inc(rope_high, 1)
            pool.wait_ge(gg_sig, 1)
            gg = z[:, Z_GG, :, :].rearrange("p t n -> p (t n)")
            link(nc.gpsimd.tensor_tensor(gg, gg, silu_nabs, ALU.mult))
            for t in range(T):
                g3 = z[:, Z_GG, t, :].rearrange("p (h v) -> p h v", h=HEADS)
                nc.gpsimd.tensor_tensor(g3, g3, g_gla_b[:, :].unsqueeze(1).broadcast_to([P, HEADS, DV]), ALU.mult).then_inc(gla_gate, 1)

        @block.tensor
        def _(pe):
            def product(v, hi, lo, k0, kn, bank, first, last, cols, before_t1=None):
                wh, wl = halfmat(w_hi, v, kn), halfmat(w_lo, v, kn)
                by_column = last and cols > NW
                for k, ns in [(k, [n]) for n in range(cols // NW) for k in range(kn)] if by_column else \
                        [(k, list(range(cols // NW))) for k in range(kn)]:
                    for t in range(T):
                        if before_t1 and k == 0 and t == 1:
                            pe.wait_ge(*before_t1)
                        sh = hi[:, k0 + k, t * P:(t + 1) * P]
                        sl = lo[:, k0 + k, t * P:(t + 1) * P]
                        for n in ns:
                            w = slice(n * NW, (n + 1) * NW)
                            nc.tensor.matmul(ps[:, bank(t, n), :], sh, wh[:, k, w], start=first and k == 0, stop=False)
                            nc.tensor.matmul(ps[:, bank(t, n), :], sh, wl[:, k, w], start=False, stop=False)
                        for n in ns:
                            w = slice(n * NW, (n + 1) * NW)
                            mm = nc.tensor.matmul(ps[:, bank(t, n), :], sl, wh[:, k, w], start=False, stop=last and k == kn - 1)
                        if by_column and (ns[0], t) != (1, T - 1):
                            mm.then_inc(cols_done, 1)
                mm.then_inc(half_used, 1)

            def first_product(v, i, bank, j=0):
                wh, wl = halfmat(w_hi, v, 2), halfmat(w_lo, v, 2)
                for a, w, start in ((act_hi, wh, True), (act_lo, wh, False), (act_hi, wl, False)):
                    if a is act_lo:
                        pe.wait_ge(act_lo_ready, 4 * i + j + 1)
                    elif w is wl:
                        pe.wait_ge(lo_done, v + 1)
                    else:
                        pe.wait_ge(act_hi_ready, 4 * i + j + 1)
                        pe.wait_ge(hi_done, v + 1)
                    for k in range(2):
                        for t in range(T):
                            mm = nc.tensor.matmul(ps[:, bank + t, :], a[:, 2 * j + k, t * P:(t + 1) * P], w[:, k, :],
                                                  start=start and j == 0 and k == 0, stop=False)
                mm.then_inc(half_used, 1)

            def transpose(i, kt, t):
                b, c = kt // 2, (kt % 2 * T + t) * P
                return nc.tensor.transpose(ps[:, T_BANK[i] + b, c:c + P], h[:, t, kt * P:(kt + 1) * P], ident[:, :])

            pe.wait_ge(zeros_ready, 1)
            for _ in range(WARM_UP):
                nc.tensor.matmul(ps[:, 7, :], zeros[:, 0:P], zeros[:, :], start=True, stop=True)
            pe.wait_ge(mix_in, 16)
            pe.wait_ge(ident_ready, 1)
            nc.tensor.transpose(ps[:, 3, 0:KT], mix_rows[:, :], ident[0:KT, 0:KT]).then_inc(gains_T, 1)
            for t in range(T):
                pe.wait_ge(x_in[t], 16)
            for b in range(4):
                for k in range(2):
                    for t in range(T):
                        mm = transpose(0, 2 * b + k, t)
                mm.then_inc(x_T, 1)

            def w_in_half(v):
                i = max(g for g in range(6) if H_GROUP[g] <= v)
                j = v - H_GROUP[i]
                if j == 0 and i >= 2:
                    pe.wait_ge(z_ready, i - 1)
                if j == 0 and i == 1:
                    pe.wait_ge(p_lo_ready, 1)
                    pe.wait_ge(gains_ready, 2)
                if j == 0 and i == 5:
                    pe.wait_ge(pp0_copied, 1)
                if i == 0:
                    pe.wait_ge(act_lo_ready, j + 1)
                pe.wait_ge(lo_done, v + 1)
                product(v, act_hi, act_lo, 2 * j, 2, lambda t, n: 2 * (i % 2) + t, j == 0, j == 3, NW)

            first_product(0, 0, 0)
            first_product(1, 0, 0, j=1)
            w_in_half(2)
            pe.wait_ge(act_lo_ready, 4)
            pe.wait_ge(ga_lo_ready, 1)
            for k in range(KT):
                nc.tensor.matmul(ps[:, 4, 0:SEQ], ga_pack[:, k, :], act_hi[:, k, :], start=k == 0, stop=False)
                mm = nc.tensor.matmul(ps[:, 4, 0:SEQ], ga_pack[:, k, :], act_lo[:, k, :], start=False, stop=k == KT - 1)
            mm.then_inc(ga_done, 1)
            pe.wait_ge(p_in, 16 * T)
            for k in range(2):
                for t in range(T):
                    mm = nc.tensor.transpose(ps[:, 2, (k * T + t) * P:(k * T + t + 1) * P], p_sb[:, t, k * P:(k + 1) * P], ident[:, :])
            mm.then_inc(p_T, 1)
            pe.wait_ge(rows_in, 16 * 2)
            nc.tensor.transpose(ps[:, 3, KT:3 * KT], gain_rows[:, :], ident[0:2 * KT, 0:2 * KT]).then_inc(gains_T, 1)
            w_in_half(3)
            pe.wait_ge(ga_copied, 1)
            pe.wait_ge(a2_in, 16 * 2)
            for t in range(T):
                mm = nc.tensor.matmul(ps[:, 5, t * 256:(t + 1) * 256], ga_T[:, t * P:(t + 1) * P], a2[:, :], start=True, stop=True)
            mm.then_inc(apre_done, 1)
            for v in (4, 5, 6):
                w_in_half(v)
            pe.wait_ge(la_lo_ready, 1)
            pe.wait_ge(triangles_ready, 2)
            for t in range(T):
                for i in range(2):
                    o = ps[:, 6 + t, i * 256:(i + 1) * 256]
                    nc.tensor.matmul(o, triangles[:, i, :], la_hi[:, t, :], start=True, stop=False)
                    nc.tensor.matmul(o, triangles[:, i, :], la_lo[:, t, :], start=False, stop=True)
            for a in range(2):
                for t in range(T):
                    mm = nc.tensor.matmul(ps[:, 4, 4 * a + 2 * t:4 * a + 2 * t + 2], la[:, t, a * P:(a + 1) * P], chunk_sum[:, :],
                                          start=True, stop=True)
            mm.then_inc(cums_done, 1)
            for v in (7, 8, 9):
                w_in_half(v)

            def head_transposes(i, bank):
                for hd in range(HEADS):
                    for t in range(T):
                        c = ((hd % 2) * T + t) * P
                        mm = nc.tensor.transpose(ps[:, bank + hd // 2, c:c + P], z[:, Z_MQ + i, t, hd * HD:(hd + 1) * HD], ident[:, :])
                mm.then_inc(qkT_done, 1)

            pe.wait_ge(qk_ready, 2)
            pe.wait_ge(decays_ready, 3)
            head_transposes(0, 4)
            for v in (10, 11, 12):
                w_in_half(v)
            w_in_half(13)
            pe.wait_ge(qk_ready, 6)
            head_transposes(1, 6)
            w_in_half(14)
            pe.wait_ge(gla_ops, 2)
            pe.wait_ge(qkT_copied, 1)
            for a in range(2):
                for t in range(T):
                    c = (a * T + t) * P
                    nc.tensor.transpose(ps[:, 4, c:c + P], dec[:, t, 0, a * P:(a + 1) * P], ident[:, :])
                    mm = nc.tensor.transpose(ps[:, 5, c:c + P], inv_dec[:, t, a * P:(a + 1) * P], ident[:, :])
            mm.then_inc(glaT_done, 1)
            w_in_half(15)

            def scores(hd):
                b = 4 + (hd + 2) % 4
                nc.tensor.matmul(ps[:, b, 0:P], q_T[:, hd, 0:P], k_T[:, hd, 0:P], start=True, stop=True)
                nc.tensor.matmul(ps[:, b, P:3 * P], q_T[:, hd, P:2 * P], k_T[:, hd, :], start=True, stop=True).then_inc(scores_done, 1)

            pe.wait_ge(qkT_copied, 2)
            scores(0)
            scores(1)
            w_in_half(16)
            pe.wait_ge(glaT_copied, 2)
            scores(2)
            scores(3)
            w_in_half(17)
            pe.wait_ge(masked, 4)
            for par in range(2):
                r = slice(par * DK, (par + 1) * DK)
                for t in range(T):
                    for a in range(2):
                        c = (t * 2 + a) * P
                        mm = nc.tensor.matmul(ps[:, 6 + par, c:c + P], ki_T[r, a, t, :], qd_T[r, a, t, :], start=True, stop=True)
                mm.then_inc(aT_done, 1)
            w_in_half(18)
            w_in_half(19)

            def pp_half(n):
                pe.wait_ge(z_ready, 4 + n)
                pe.wait_ge(lo_done, H_PP + n + 1)
                product(H_PP + n, p_hi, p_lo, 0, 2, lambda t, _: 2 * (1 - n) + t, True, True, NW)

            pp_half(0)
            pe.wait_ge(z_ready, 5)
            pe.wait_ge(gla_ops, 3)
            pe.wait_ge(aT_masked, 2)
            for n in range(3):
                t, r = n // 2, slice((n % 2) * CHUNK, (n % 2 + 1) * CHUNK)
                bank, c0 = (7, 0) if n == 1 else (6, 256 * (n // 2))
                for hd in range(HEADS):
                    a, par = hd // 2, hd % 2
                    mm = nc.tensor.matmul(ps[par * DK:(par + 1) * DK, bank, c0 + a * DV:c0 + (a + 1) * DV],
                                          dec[r, t, 1, hd * DK:(hd + 1) * DK], z[r, Z_GV, t, hd * DV:(hd + 1) * DV],
                                          start=True, stop=True)
            mm.then_inc(ds_done, 1)
            pp_half(1)
            pe.wait_ge(states_ready, 1)
            pe.wait_ge(masked, 8)
            for par in range(2):
                r = slice(par * DK, (par + 1) * DK)
                for t in range(T):
                    for a in range(2):
                        hd = 2 * a + par
                        c = (t * 2 + a) * DV
                        nc.tensor.matmul(ps[:, 4 + par, c:c + DV], a_T[:, par, t, a, :], z[:, Z_GV, t, hd * DV:(hd + 1) * DV],
                                         start=True, stop=True)
                        for m in range(2):
                            n = 2 * t + m
                            if n:
                                mm = nc.tensor.matmul(ps[m * CHUNK:(m + 1) * CHUNK, 4 + par, c:c + DV],
                                                      qd_T[r, a, t, m * CHUNK:(m + 1) * CHUNK], state[r, n - 1, a, :],
                                                      start=False, stop=True, skip_group_check=True)
            mm.then_inc(o_done, 1)
            w_in_half(22)

            def prob_transposes(i):
                pe.wait_ge(probs_ready, i + 1)
                for hd in (2 * i, 2 * i + 1):
                    for m in range(3):
                        mm = nc.tensor.transpose(ps[:, 6 + hd % 2, m * P:(m + 1) * P], probs[:, hd, m * P:(m + 1) * P], ident[:, :])
                mm.then_inc(pT_done, 1)

            prob_transposes(0)
            w_in_half(23)
            pe.wait_ge(pT_copied, 1)
            prob_transposes(1)
            w_in_half(24)
            pe.wait_ge(o_ready, 2)
            for hd in range(HEADS):
                for t in range(T):
                    c = ((hd % 2) * T + t) * P
                    mm = nc.tensor.transpose(ps[:, 4 + hd // 2, c:c + P], o_gla[:, t, hd * DV:(hd + 1) * DV], ident[:, :])
            mm.then_inc(oT_done, 1)
            w_in_half(25)
            pe.wait_ge(pp1_copied, 1)

            def w_out_half(j, before_t1=None):
                if j in (0, 4):
                    pe.wait_ge(mix_lo_ready, 2 if j == 0 else 4)
                pe.wait_ge(lo_done, H_OUT + j + 1)
                product(H_OUT + j, mix_hi, mix_lo, j, 1, lambda t, n: 2 * t + n, j == 0, j == KT - 1, D, before_t1)

            w_out_half(0, (z_ready, 6))
            pe.wait_ge(pT_copied, 2)
            for hd in range(HEADS):
                d = slice(hd * HD, (hd + 1) * HD)
                c = (hd % 2) * SEQ
                nc.tensor.matmul(ps[:, 6 + hd // 2, c:c + SEQ], z[:, Z_MV, 0, d], probs_T[:, hd, 0:SEQ], start=True, stop=True)
                mm = nc.tensor.matmul(ps[:, 6 + hd // 2, c + P:c + SEQ], z[:, Z_MV, 1, d], probs_T[:, hd, SEQ:SEQ + P],
                                      start=False, stop=True, skip_group_check=True)
            mm.then_inc(pv_done, 1)
            for j in range(1, KT):
                w_out_half(j)

            def residual_transposes(i):
                for n in range(2):
                    for t in range(T):
                        pe.wait_ge(h_ready, 4 * (i - 1) + 2 * n + t + 1)
                        for b in (2 * n, 2 * n + 1):
                            for k in range(2):
                                mm = transpose(i, 2 * b + k, t)
                            if t == T - 1:
                                mm.then_inc(x_T, 1)

            residual_transposes(1)
            first_product(H_UP0, 1, 2)
            for j in range(1, 4):
                pe.wait_ge(act_lo_ready, 4 + j + 1)
                pe.wait_ge(lo_done, H_UP0 + j + 1)
                product(H_UP0 + j, act_hi, act_lo, 2 * j, 2, lambda t, n: 2 + t, False, j == 3, NW)

            def hidden_transposes(g):
                for t in range(T):
                    pe.wait_ge(squared, T * g + (t + 1 - T))
                    for b in range(2):
                        for k in range(2):
                            kt = 2 * b + k
                            mm = nc.tensor.transpose(ps[:, 2 + b, (k * T + t) * P:(k * T + t + 1) * P],
                                                     hidden[:, t, kt * P:(kt + 1) * P], ident[:, :])
                        if t == T - 1:
                            mm.then_inc(hidT_done, 1)

            def down(g, v0, lo_wait, k0=0, first=False, last=False, between=None):
                for j in range(4):
                    if j % 2 == 0:
                        pe.wait_ge(hid_lo, 2 * g - 1 + j // 2)
                    if j == 2 and between:
                        between()
                    pe.wait_ge(lo_done, lo_wait + j)
                    product(v0 + j, mix_hi, mix_lo, k0 + j, 1, lambda t, n: 4 + 2 * t + n, first and j == 0, last and j == 3, D)

            def ffn_group(g, first=False, between=None):
                for j in range(4):
                    if j == (1 if first else 0):
                        if first:
                            pe.wait_ge(relu_done, T)
                        hidden_transposes(g)
                    pe.wait_ge(lo_done, LOOP_HALVES * g + (H_LOOP + j + 1 - LOOP_HALVES))
                    product(H_LOOP + j, act_hi, act_lo, 2 * j, 2, lambda t, n: t, j == 0, j == 3, NW)
                down(g, H_LOOP + 4, LOOP_HALVES * g + (H_LOOP + 5 - LOOP_HALVES), first=first, between=between)

            ffn_group(1, first=True)
            with pe.Fori(2, GROUPS - 1) as g:
                ffn_group(g)
            ffn_group(GROUPS - 1, between=lambda: hidden_transposes(GROUPS))
            down(GROUPS, H_DOWN_LAST, H_DOWN_LAST + 1, k0=4, last=True)
            residual_transposes(2)
            for n in range(2):
                for j in range(4):
                    v = H_GATE + 4 * n + j
                    if v == H_GATE:
                        first_product(v, 2, 4)
                        continue
                    if n == 0:
                        pe.wait_ge(act_lo_ready, 8 + j + 1)
                    pe.wait_ge(lo_done, v + 1)
                    if v < H_END - 2:
                        product(v, act_hi, act_lo, 2 * j, 2, lambda t, _: 4 + 2 * n + t, j == 0, j == 3, NW)
            for t in range(T):
                o = ps[:, 6 + t, :]
                for k in range(4):
                    v = H_END - 2 + k // 2
                    wh, wl = halfmat(w_hi, v, 2)[:, k % 2, :], halfmat(w_lo, v, 2)[:, k % 2, :]
                    sh, sl = (a[:, KT - 4 + k, t * P:(t + 1) * P] for a in (act_hi, act_lo))
                    nc.tensor.matmul(o, sh, wh, start=False, stop=False)
                    nc.tensor.matmul(o, sh, wl, start=False, stop=False)
                    mm = nc.tensor.matmul(o, sl, wh, start=False, stop=k == 3)
                mm.then_inc(tile_done, 1)


_INS = ["x", "p", "positions", "g_mix", "w_in", "w_gla_a2", "b_gla_a", "g_gla_out", "g_moba_q", "g_moba_k", "w_out",
        "g_ffn", "w_up", "w_down", "g_ple_gate", "w_ple_gate", "w_ple_proj", "g_ple_emb"]


def kernel(**inputs):
    import numpy as np
    import concourse.bacc as bacc
    from concourse.bass_utils import run_bass_kernel_spmd

    nc = bacc.Bacc("TRN2", target_bir_lowering=False, num_devices=1)
    arrays, args = {}, []

    def add(name, a):
        arrays[name] = a
        args.append(nc.dram_tensor(name, a.shape, mybir.dt.from_np(a.dtype), kind="ExternalInput").ap())

    for name in _INS:
        a = np.ascontiguousarray(inputs[name])
        while a.ndim > 1 and a.shape[0] == 1:
            a = a[0]
        add("in_" + name, a)
    half = HD // 2
    add("inv_freq", (np.float32(1.0) / np.float32(10000.0) ** (np.arange(half, dtype=np.float32) / np.float32(half))).astype(np.float32))
    args.append(nc.dram_tensor("out", (SEQ, D), F32, kind="ExternalOutput").ap())
    build(nc, *args)
    r = run_bass_kernel_spmd(nc, [arrays], core_ids=[0])
    return r.results[0]["out"].reshape(1, SEQ, D)
```
